# Optimizing a Trainium2 kernel written in Bass

```python
import math
import jax, jax.numpy as jnp
from jax import lax
import numpy as np

D_MODEL = 1024
BATCH = 1
SEQ = 256
DEPTH = 2

ATT_HEADS = 8
ATT_HEAD_DIM = 64
ATT_V_DIM = 2 * ATT_HEAD_DIM
ROPE_DIM = ATT_HEAD_DIM // 4
ROPE_THETA = 500000.0
Q_BLOCK = 128
SSM_INNER = 2 * D_MODEL
SSM_HEAD_DIM = 64
SSM_HEADS = SSM_INNER // SSM_HEAD_DIM
SSM_GROUPS = 8
SSM_STATE = 128
SSM_CONV = 5
SSM_CHUNK = 128
DT_MIN = 0.001
DT_MAX = 0.1
PEER_HEADS = 8
PEER_KEYS = 128
PEER_EXPERTS = PEER_KEYS * PEER_KEYS
PEER_KEY_DIM = 256
PEER_HALF = PEER_KEY_DIM // 2
PEER_TOPK = 16
PEER_BLOCK = 128

RMS_EPS = 1e-6

Q_COLS = ATT_HEADS * 2 * ATT_HEAD_DIM
K_COLS = ATT_HEADS * 2 * ATT_HEAD_DIM
V_COLS = ATT_HEADS * ATT_V_DIM
Z_COLS = SSM_INNER
XBC_COLS = SSM_INNER + 2 * SSM_GROUPS * SSM_STATE
DT_COLS = 2 * SSM_HEADS
GATE_COLS = 2 * D_MODEL
IN_COLS = Q_COLS + K_COLS + V_COLS + Z_COLS + XBC_COLS + DT_COLS + GATE_COLS
SPLIT_POINTS = (Q_COLS,
                Q_COLS + K_COLS,
                Q_COLS + K_COLS + V_COLS,
                Q_COLS + K_COLS + V_COLS + Z_COLS,
                Q_COLS + K_COLS + V_COLS + Z_COLS + XBC_COLS,
                Q_COLS + K_COLS + V_COLS + Z_COLS + XBC_COLS + DT_COLS)

kernel_name = "hybrid_diffattn_ssd_peer_encoder"

def rmsnorm(x, g):
    xf = x.astype(jnp.float32)
    y = xf * lax.rsqrt(jnp.mean(xf * xf, axis=-1, keepdims=True) + RMS_EPS)
    return y.astype(x.dtype) * g

def rotary_tables(positions, dtype):
    inv_freq = ROPE_THETA ** (-jnp.arange(0, ROPE_DIM, 2, dtype=jnp.float32) / ROPE_DIM)
    ang = positions.astype(jnp.float32)[..., None] * inv_freq
    cos = jnp.cos(ang)[:, :, None, None, :].astype(dtype)
    sin = jnp.sin(ang)[:, :, None, None, :].astype(dtype)
    return cos, sin

def partial_rotary(t, cos, sin):
    half = ROPE_DIM // 2
    r1, r2, rest = t[..., :half], t[..., half:ROPE_DIM], t[..., ROPE_DIM:]
    return jnp.concatenate([r1 * cos - r2 * sin, r2 * cos + r1 * sin, rest], axis=-1)

def diff_attention(q, k, v, lam):
    b, s, h, _, d = q.shape
    scale = d ** -0.5
    nq = s // Q_BLOCK
    qb = q.reshape(b, nq, Q_BLOCK, h, 2, d).transpose(1, 0, 2, 3, 4, 5)

    def block(qblk):
        sc = jnp.einsum('bqhcd,bkhcd->bhcqk', qblk, k).astype(jnp.float32) * scale
        p = jax.nn.softmax(sc, axis=-1)
        w = p[:, :, 0] - lam * p[:, :, 1]
        return jnp.einsum('bhqk,bkhe->bqhe', w.astype(v.dtype), v)

    out = lax.map(block, qb)
    return out.transpose(1, 0, 2, 3, 4).reshape(b, s, h, 2 * d)

def centred_dwconv(u, w, bias):
    width, ch = w.shape
    out = lax.conv_general_dilated(
        u, w[:, None, :].astype(u.dtype), window_strides=(1,),
        padding=[(width // 2, width // 2)],
        dimension_numbers=('NWC', 'WIO', 'NWC'), feature_group_count=ch)
    return out + bias

def segsum(a):
    t = a.shape[-1]
    cs = jnp.cumsum(a, axis=-1)
    diff = cs[..., :, None] - cs[..., None, :]
    mask = jnp.tril(jnp.ones((t, t), dtype=bool))
    return jnp.where(mask, diff, -jnp.inf)

def ssd_scan(x, dt, a_neg, bm, cm):
    b, l, h, p = x.shape
    g, n = bm.shape[-2:]
    r = h // g
    c = l // SSM_CHUNK
    q = SSM_CHUNK
    xs = (x.astype(jnp.float32) * dt[..., None]).reshape(b, c, q, g, r, p)
    a = (dt * a_neg).reshape(b, c, q, g, r).transpose(0, 3, 4, 1, 2)
    bc = bm.reshape(b, c, q, g, n)
    cc = cm.reshape(b, c, q, g, n)
    a_cs = jnp.cumsum(a, axis=-1)
    decay_in = jnp.exp(segsum(a))
    cb = jnp.einsum('bclgn,bcsgn->bgcls', cc, bc)
    y_diag = jnp.einsum('bgrcls,bcsgrp->bclgrp', cb[:, :, None] * decay_in, xs)
    decay_states = jnp.exp(a_cs[..., -1:] - a_cs).transpose(0, 3, 4, 1, 2)
    states = jnp.einsum('bclgn,bclgrp->bcgrpn', bc, xs * decay_states[..., None])
    chunk_a = jnp.pad(a_cs[..., -1], ((0, 0), (0, 0), (0, 0), (1, 0)))
    decay_chunk = jnp.exp(segsum(chunk_a))
    states0 = jnp.concatenate([jnp.zeros_like(states[:, :1]), states], axis=1)
    entry = jnp.einsum('bgrzc,bcgrpn->bzgrpn', decay_chunk, states0)[:, :-1]
    decay_out = jnp.exp(a_cs).transpose(0, 3, 4, 1, 2)
    y_off = jnp.einsum('bclgn,bcgrpn->bclgrp', cc, entry) * decay_out[..., None]
    return (y_diag + y_off).reshape(b, l, h, p).astype(x.dtype)

def mamba2_bidir(z, xbc, dt_raw, conv_w, conv_b, dt_bias, a_log, d_skip, norm_g):
    b, s, _ = z.shape
    xbc = jax.nn.silu(centred_dwconv(xbc, conv_w, conv_b))
    xs, bm, cm = jnp.split(xbc, [SSM_INNER, SSM_INNER + SSM_GROUPS * SSM_STATE], axis=-1)
    xs = xs.reshape(b, s, SSM_HEADS, SSM_HEAD_DIM)
    bm = bm.reshape(b, s, SSM_GROUPS, SSM_STATE)
    cm = cm.reshape(b, s, SSM_GROUPS, SSM_STATE)
    dt = jax.nn.softplus(dt_raw.astype(jnp.float32).reshape(b, s, 2, SSM_HEADS)
                         + dt_bias.astype(jnp.float32))
    a_neg = -jnp.exp(a_log.astype(jnp.float32))
    y_fwd = ssd_scan(xs, dt[:, :, 0], a_neg[0], bm, cm)
    y_bwd = ssd_scan(xs[:, ::-1], dt[:, ::-1, 1], a_neg[1], bm[:, ::-1], cm[:, ::-1])[:, ::-1]
    y = (y_fwd + y_bwd + d_skip[:, None] * xs).reshape(b, s, SSM_INNER)
    return rmsnorm(y * jax.nn.silu(z), norm_g)

def peer_ffn(h, wq, keys, u_tab, v_tab):
    b, s, d = h.shape
    qry = (h @ wq).reshape(b, s, PEER_HEADS, 2, PEER_HALF)
    sc = jnp.einsum('bshcd,hckd->bshck', qry, keys).astype(jnp.float32)
    v1, i1 = lax.top_k(sc[..., 0, :], PEER_TOPK)
    v2, i2 = lax.top_k(sc[..., 1, :], PEER_TOPK)
    cand = (v1[..., :, None] + v2[..., None, :]).reshape(b, s, PEER_HEADS, PEER_TOPK * PEER_TOPK)
    cand_idx = (i1[..., :, None] * PEER_KEYS + i2[..., None, :]).reshape(b, s, PEER_HEADS, PEER_TOPK * PEER_TOPK)
    best, pos = lax.top_k(cand, PEER_TOPK)
    idx = jnp.take_along_axis(cand_idx, pos, axis=-1)
    gate = jax.nn.softmax(best, axis=-1)
    nb = s // PEER_BLOCK
    hk = PEER_HEADS * PEER_TOPK
    hb = h.reshape(b, nb, PEER_BLOCK, d).transpose(1, 0, 2, 3)
    ib = idx.reshape(b, nb, PEER_BLOCK, hk).transpose(1, 0, 2, 3)
    gb = gate.reshape(b, nb, PEER_BLOCK, hk).transpose(1, 0, 2, 3)

    def expert_block(args):
        hx, ix, gx = args
        u = jnp.take(u_tab, ix, axis=0)
        act = jax.nn.gelu(jnp.einsum('btkd,btd->btk', u, hx).astype(jnp.float32), approximate=False)
        wgt = (act * gx).astype(hx.dtype)
        return jnp.einsum('btk,btkd->btd', wgt, jnp.take(v_tab, ix, axis=0))

    out = lax.map(expert_block, (hb, ib, gb))
    return out.transpose(1, 0, 2, 3).reshape(b, s, d)

def setup_inputs(seed: int = 0) -> dict:
    key = jax.random.key(seed)
    ks = jax.random.split(key, 24)
    f32 = jnp.float32

    def nrm(k, shape, scale):
        return jax.random.normal(k, shape, f32) * scale

    def gain(k, shape):
        return 1.0 + 0.02 * jax.random.normal(k, shape, f32)

    x = nrm(ks[0], (BATCH, SEQ, D_MODEL), 1.0)
    offsets = jax.random.randint(ks[1], (BATCH, 1), 0, 4096, dtype=jnp.int32)
    positions = offsets + jnp.arange(SEQ, dtype=jnp.int32)[None, :]
    norm1_g = gain(ks[2], (DEPTH, D_MODEL))
    w_in = nrm(ks[3], (DEPTH, D_MODEL, IN_COLS), D_MODEL ** -0.5)
    gate_b = nrm(ks[4], (DEPTH, GATE_COLS), 0.01)
    diff_lam = nrm(ks[5], (DEPTH, 4, ATT_HEAD_DIM), 0.1)
    subln_g = gain(ks[6], (DEPTH, ATT_V_DIM))
    w_att_br = nrm(ks[7], (DEPTH, V_COLS, D_MODEL), V_COLS ** -0.5)
    conv_w = nrm(ks[8], (DEPTH, SSM_CONV, XBC_COLS), SSM_CONV ** -0.5)
    conv_b = nrm(ks[9], (DEPTH, XBC_COLS), 0.01)
    u = jax.random.uniform(ks[10], (DEPTH, 2, SSM_HEADS), f32)
    dt0 = jnp.exp(u * (math.log(DT_MAX) - math.log(DT_MIN)) + math.log(DT_MIN))
    dt_bias = dt0 + jnp.log(-jnp.expm1(-dt0))
    a_log = jnp.log(jax.random.uniform(ks[11], (DEPTH, 2, SSM_HEADS), f32, 1.0, 16.0))
    d_skip = gain(ks[12], (DEPTH, SSM_HEADS))
    ssm_norm_g = gain(ks[13], (DEPTH, SSM_INNER))
    w_ssm_br = nrm(ks[14], (DEPTH, SSM_INNER, D_MODEL), SSM_INNER ** -0.5)
    w_out = nrm(ks[15], (DEPTH, D_MODEL, D_MODEL), D_MODEL ** -0.5)
    norm2_g = gain(ks[16], (DEPTH, D_MODEL))
    peer_wq = nrm(ks[17], (DEPTH, D_MODEL, PEER_HEADS * PEER_KEY_DIM), D_MODEL ** -0.5)
    peer_keys = nrm(ks[18], (DEPTH, PEER_HEADS, 2, PEER_KEYS, PEER_HALF), PEER_HALF ** -0.5)
    peer_u = nrm(ks[19], (DEPTH, PEER_EXPERTS, D_MODEL), D_MODEL ** -0.5)
    peer_v = nrm(ks[20], (DEPTH, PEER_EXPERTS, D_MODEL), PEER_TOPK ** -0.5)
    final_g = gain(ks[21], (D_MODEL,))
    return {"x": x, "positions": positions, "norm1_g": norm1_g, "w_in": w_in,
            "gate_b": gate_b, "diff_lam": diff_lam, "subln_g": subln_g,
            "w_att_br": w_att_br, "conv_w": conv_w, "conv_b": conv_b,
            "dt_bias": dt_bias, "a_log": a_log, "d_skip": d_skip,
            "ssm_norm_g": ssm_norm_g, "w_ssm_br": w_ssm_br, "w_out": w_out,
            "norm2_g": norm2_g, "peer_wq": peer_wq, "peer_keys": peer_keys,
            "peer_u": peer_u, "peer_v": peer_v, "final_g": final_g}

def reference(x, positions, norm1_g, w_in, gate_b, diff_lam, subln_g, w_att_br,
              conv_w, conv_b, dt_bias, a_log, d_skip, ssm_norm_g, w_ssm_br, w_out,
              norm2_g, peer_wq, peer_keys, peer_u, peer_v, final_g):
    b, s, _ = x.shape
    cos, sin = rotary_tables(positions, x.dtype)
    for l in range(DEPTH):
        lam_init = 0.8 - 0.6 * math.exp(-0.3 * l)
        h = rmsnorm(x, norm1_g[l])
        proj = h @ w_in[l]
        q, k, v, z, xbc, dt_raw, gate_logits = jnp.split(proj, SPLIT_POINTS, axis=-1)
        q = partial_rotary(q.reshape(b, s, ATT_HEADS, 2, ATT_HEAD_DIM), cos, sin)
        k = partial_rotary(k.reshape(b, s, ATT_HEADS, 2, ATT_HEAD_DIM), cos, sin)
        v = v.reshape(b, s, ATT_HEADS, ATT_V_DIM)
        lp = diff_lam[l].astype(jnp.float32)
        lam = jnp.exp(jnp.sum(lp[0] * lp[1])) - jnp.exp(jnp.sum(lp[2] * lp[3])) + lam_init
        att = rmsnorm(diff_attention(q, k, v, lam), subln_g[l]) * (1.0 - lam_init)
        a_out = att.reshape(b, s, V_COLS) @ w_att_br[l]
        m = mamba2_bidir(z, xbc, dt_raw, conv_w[l], conv_b[l], dt_bias[l], a_log[l],
                         d_skip[l], ssm_norm_g[l])
        m_out = m @ w_ssm_br[l]
        g_att, g_ssm = jnp.split(jax.nn.sigmoid(gate_logits + gate_b[l]), 2, axis=-1)
        x = x + (g_att * a_out + g_ssm * m_out) @ w_out[l]
        x = x + peer_ffn(rmsnorm(x, norm2_g[l]), peer_wq[l], peer_keys[l], peer_u[l], peer_v[l])
    return rmsnorm(x, final_g)


_drawn_inputs = setup_inputs


def setup_inputs(seed=0):
    import zlib

    import numpy as np

    out = dict(_drawn_inputs(seed))
    spreads = {}
    factors = {'gate_b': 6.085,
     'subln_g': 7.981,
     'conv_b': 3.12,
     'd_skip': 14.338,
     'ssm_norm_g': 7.365,
     'final_g': 7.59,
     'norm2_g': 4.767}
    for name, (base, spread) in spreads.items():
        noise = np.random.default_rng([zlib.crc32(name.encode()), seed]).standard_normal(out[name].shape)
        drawn = base * np.exp(spread * noise) if base else spread * noise
        out[name] = __import__('jax').numpy.asarray(drawn.astype(out[name].dtype))
    for name, factor in factors.items():
        out[name] = (out[name] * factor).astype(out[name].dtype)
    return out
```

```python
import math
from contextlib import ExitStack

import numpy as np
import concourse.bass as bass
from concourse import mybir

F32 = mybir.dt.float32
U32 = mybir.dt.uint32
I32 = mybir.dt.int32
ALU = mybir.AluOpType
ACT = mybir.ActivationFunctionType
AX = mybir.AxisListType

DEPTH, SEQ, DM = 2, 256, 1024
P = 128
TB = SEQ // P
KD = DM // P
HEADS, HD, VD = 8, 64, 128
ROPE = HD // 4
THETA = 500000.0
INNER, SH, SP_, GROUPS, STATE, CONV = 2048, 32, 64, 8, 128, 5
HPG = SH // GROUPS
XT = INNER // P
NXBC = (INNER + 2 * GROUPS * STATE) // P
PH, PK, TOPK = 8, 128, 16
EXPERTS = PK * PK
SLOTS = PH * TOPK
EPS = 1e-6
NEG = -3.0e38

C_XBC, C_QK, C_Z, C_GATE, C_V, C_ATT, C_SSM, C_OUT, C_WQ, CHUNKS = 0, 8, 12, 16, 20, 22, 24, 28, 30, 34

PARAM_SIZES = [("n1g", KD), ("n2g", KD), ("sng", XT), ("cw", NXBC * CONV), ("cb", NXBC), ("gb", 2 * KD),
               ("sub", 1), ("dsk", XT), ("dtb", 2 * SH), ("alog", 2 * SH), ("lam", 4 * HD), ("laminit", 1), ("row0", 1)]
PARAM = {}
_at = 0
for _n, _s in PARAM_SIZES:
    PARAM[_n] = (_at, _at + _s)
    _at += _s
NPAR = _at

CONST_SIZES = [("ident", P), ("tri_le", P), ("tri_ge", P), ("ones", P), ("prot", P), ("iota", TOPK), ("freq", 1)]
CONST = {}
_at = 0
for _n, _s in CONST_SIZES:
    CONST[_n] = (_at, _at + _s)
    _at += _s
NCONST = _at

RING = 16
QUAD = 4
QUADS = RING // QUAD
WAVES = SLOTS // RING

LOG_TERMS = [1.0 / (2 * k + 1) for k in range(8, 0, -1)]


class Count:

    def __init__(self, sem, per_layer):
        self.sem, self.per_layer = sem, per_layer

    def at(self, layer, n):
        return layer * self.per_layer + n


class Steps:

    def __init__(self, eng, count, layer):
        self.eng, self.count, self.layer, self.n = eng, count, layer, 0

    def do(self, ins):
        self.n += 1
        ins.then_inc(self.count.sem, 1)

    def wait(self):
        self.eng.wait_ge(self.count.sem, self.count.at(self.layer, self.n))


def bc(ap, axis, n):
    shape = list(ap.shape)
    shape.insert(axis, n)
    return ap.unsqueeze(axis).broadcast_to(shape)


def encoder_kernel(nc, x, positions, consts, params, w_stream, w_dt, keys_t, norm2_rows, final_row,
                   peer_u, peer_v, out):
    with ExitStack() as ctx:
        base = [(nc.sbuf_base + 63) // 64 * 64]
        end = nc.sbuf_usable_end

        def place(at, name, shape, dt=F32):
            size = int(np.prod(shape[1:])) * 4
            assert at + size <= end, (name, at + size, end)
            return nc.alloc_sbuf_tensor_at(name, shape, dt, offset=at), (at + size + 31) // 32 * 32

        def fixed(name, shape, dt=F32):
            t, base[0] = place(base[0], name, shape, dt)
            return t

        x_tok = fixed("x_tok", [P, TB, DM])
        hT = fixed("hT", [P, KD, SEQ])
        w_ring = fixed("w_ring", [P, 2, 4096])
        cst = fixed("cst", [P, NCONST])
        cos_t = fixed("cos_t", [P, SEQ])
        sin_t = fixed("sin_t", [P, SEQ])
        par_all = fixed("par_all", [P, DEPTH, NPAR])
        par = fixed("par", [P, NPAR])
        wdt_all = fixed("wdt_all", [P, DEPTH, KD * 2 * SH])
        ssq = fixed("ssq", [P, TB])
        rms = fixed("rms", [P, TB])
        rstd = fixed("rstd", [P, TB])
        mx = fixed("mx", [P, 2, 2, TB])
        nb = fixed("nb", [P, 2, 2, TB])
        sums = fixed("sums", [P, 2, 2, TB])
        rec = fixed("rec", [P, 2, 2, TB])
        lam2 = fixed("lam2", [P, 2])
        neglam = fixed("neglam", [P, 1])
        subg = fixed("subg", [P, 1])
        aneg = fixed("aneg", [P, 2 * SH])
        lamp = fixed("lamp", [P, 2, HD])
        ossq = fixed("ossq", [P, TB * HEADS])

        def const(name):
            return cst[:, CONST[name][0]:CONST[name][1]]

        def param(name, i=0, n=None):
            a = PARAM[name][0] + i
            return par[:, a:(PARAM[name][1] if n is None else a + n)]

        ident, tri_le, tri_ge, ones = const("ident"), const("tri_le"), const("tri_ge"), const("ones")

        arena = base[0]
        at = arena
        xbc, at = place(at, "xbc", [P, NXBC, SEQ])
        qk, at = place(at, "qk", [P, 2 * HEADS, SEQ])
        x_fwd, _ = place(at - 2 * HEADS * SEQ * 4, "x_fwd", [P, TB, INNER])
        attT, _ = place(at, "attT", [P, KD, SEQ])
        x_bwd, _ = place(at, "x_bwd", [P, TB, INNER])
        v_tok, at = place(at + KD * SEQ * 4, "v_tok", [P, TB, DM])
        zT, at = place(at, "zT", [P, XT, SEQ])
        gateT, at = place(at, "gateT", [P, 2 * KD, SEQ])
        temps = at
        m_mat, at = place(at, "m_mat", [P, 2, 6, HPG, P])
        cbm, at = place(at, "cbm", [P, 2, 6, P])
        a_tri, at = place(at, "a_tri", [P, 4, HPG, P])
        y_grp, at = place(at, "y_grp", [P, 2, TB, HPG * SP_])
        dt_v, at = place(at, "dt_v", [P, TB, 2 * SH])
        a_v, at = place(at, "a_v", [P, TB, 2 * SH])
        f_col, at = place(at, "f_col", [P, TB, 2 * SH])
        off_b, at = place(at, "off_b", [P, 2 * SH])
        sp, at2 = place(temps + 16384, "sp", [P, 6, TB * 2 * SH])
        c_tmp, at2 = place(at2, "c_tmp", [P, 2, 2, SEQ])
        xn, _ = place(temps, "xn", [P, TB, DM])
        rot_tmp, at2 = place(at2, "rot_tmp", [P, 2, SEQ])
        e_buf, a3 = place(temps, "e_buf", [P, 2, 2, TB, SEQ])
        wT, a3 = place(a3, "wT", [P, 2, TB, SEQ])
        o_sq, a3 = place(temps, "o_sq", [P, TB * HEADS, VD])
        s_tmp, a3 = place(temps, "s_tmp", [P, 4, SEQ])
        y_sq2, _ = place(temps, "y_sq2", [P, 2, 2, SEQ])
        r_bc, _ = place(temps + 8192, "r_bc", [P, SEQ])
        trig, _ = place(temps, "trig", [P, 4, SEQ])
        pos_i, _ = place(temps + 8192, "pos_i", [P, SEQ], I32)
        o_view = hT[:].rearrange("p k t -> p (k t)").rearrange("p (b h e) -> p b h e", b=TB, h=HEADS)

        at = arena
        ring, at = place(at, "ring", [P, RING, DM])
        sc, at = place(at, "sc", [P, TB, 2 * PH, PK])
        h2, at = place(at, "h2", [P, TB, DM])
        keys, at = place(at, "keys", [P, 2 * PH, PK])
        qryT, _ = place(at, "qryT", [P, 2 * PH, SEQ])
        cand, at = place(at, "cand", [P, PH, TOPK, TOPK])
        eq, at = place(at, "eq", [P, PH, TOPK, TOPK])
        g2row, at = place(at, "g2row", [P, DM])
        vals, at = place(at, "vals", [P, TB, 2 * PH, TOPK])
        idxs, at = place(at, "idxs", [P, TB, 2 * PH, TOPK], U32)
        best, at = place(at, "best", [P, TB, PH, TOPK])
        posn, at = place(at, "posn", [P, TB, PH, TOPK], U32)
        idxf, at = place(at, "idxf", [P, 2 * PH, TOPK])
        ab_u, at = place(at, "ab_u", [P, 2, SLOTS], U32)
        ab_f, at = place(at, "ab_f", [P, 2, SLOTS])
        selv, at = place(at, "selv", [P, 2, SLOTS])
        ex_i, at = place(at, "ex_i", [P, TB, SLOTS], U32)
        gsum, at = place(at, "gsum", [P, TB, PH])
        gate_w, at = place(at, "gate_w", [P, TB, PH, TOPK])
        act_u, at = place(at, "act_u", [P, TB, SLOTS])
        gel, at = place(at, "gel", [P, TB, SLOTS])
        wgt, at = place(at, "wgt", [P, TB, SLOTS])
        stage, at = place(at, "stage", [P, 2, RING], U32)
        diag, at = place(at, "diag", [P, 3, P])
        acc_v, at = place(at, "acc_v", [P, DM])

        bank = [ctx.enter_context(nc.psum_tensor(f"bank{i}", [P, 512], F32)) for i in range(8)]

        def two(b):
            return bank[b][:].rearrange("p (j t) -> p j t", j=2)

        def once(name):
            return ctx.enter_context(nc.semaphore(name))

        def sem(name, per_layer):
            return Count(once(name), per_layer)

        setup_loaded = once("setup_loaded")
        chunk_loaded = [sem(f"chunk_loaded{i}", 16 * CHUNKS // 2) for i in range(2)]
        chunk_begun = sem("chunk_begun", CHUNKS)
        tables_ready = once("tables_ready")
        trig_step = once("trig_step")
        trig_ready = once("trig_ready")
        par_ready = sem("par_ready", 1)
        x_ready = sem("x_ready", TB)
        alog_exp = sem("alog_exp", 1)
        sq_done = sem("sq_done", 2)
        ms_ready = sem("ms_ready", 2)
        rms_ready = sem("rms_ready", 2)
        xn_ready = sem("xn_ready", 2)
        STREAM = 4 + 40 + 4 + 4 + 4 + 8 + 8
        bank_full = sem("bank_full", STREAM)
        bank_empty = sem("bank_empty", STREAM)
        conv_taps = sem("conv_taps", NXBC // 2 * CONV)
        xbc_ready = sem("xbc_ready", NXBC // 2)
        dt_proj = sem("dt_proj", 1)
        dt_act = sem("dt_act", 2)
        dt_abs_in = sem("dt_abs_in", 1)
        a_ready = sem("a_ready", 1)
        cums_done = sem("cums_done", 1)
        cums_copied = sem("cums_copied", 1)
        rot_full = sem("rot_full", HEADS)
        rot_empty = sem("rot_empty", HEADS)
        lam_in = sem("lam_in", 1)
        lam_exp = sem("lam_exp", 1)
        sc_done = sem("sc_done", HEADS)
        nb_ready = sem("nb_ready", HEADS)
        exp_done = sem("exp_done", HEADS)
        w_ready = sem("w_ready", HEADS)
        w_turned = sem("w_turned", HEADS)
        wT_ready = sem("wT_ready", HEADS)
        av_done = sem("av_done", HEADS)
        o_copied = sem("o_copied", HEADS)
        oms_ready = sem("oms_ready", 1)
        orms_ready = sem("orms_ready", 1)
        att_normed = sem("att_normed", 1)
        mix_full = sem("mix_full", 4 + 4 + 4)
        mix_empty = sem("mix_empty", 4 + 4 + 4)
        xt_full = sem("xt_full", 8)
        xt_empty = sem("xt_empty", 8)
        atri_ready = sem("atri_ready", 4 * GROUPS)
        f_done = sem("f_done", 4 * GROUPS)
        cb_done = sem("cb_done", GROUPS)
        diff_ready = sem("diff_ready", 4 * GROUPS)
        offexp_done = sem("offexp_done", 2 * GROUPS)
        cboff_copied = sem("cboff_copied", GROUPS)
        cb_masked = sem("cb_masked", GROUPS)
        dec_exp = sem("dec_exp", 4 * GROUPS)
        m_ready = sem("m_ready", GROUPS)
        y_done = sem("y_done", GROUPS)
        y_copied = sem("y_copied", GROUPS)
        y_turned = sem("y_turned", GROUPS)
        yz_ready = sem("yz_ready", GROUPS)
        ysq_ready = sem("ysq_ready", XT // 2)
        ysq_used = sem("ysq_used", XT // 2)
        yms_ready = sem("yms_ready", 1)
        yrms_ready = sem("yrms_ready", 1)
        m_scaled = sem("m_scaled", 1)
        peer_loaded = sem("peer_loaded", 32)
        h2_ready = sem("h2_ready", 1)
        sc_copied = sem("sc_copied", 8)
        best_shift = sem("best_shift", TB)
        best_exp = sem("best_exp", TB)
        experts_ready = sem("experts_ready", TB)
        WAVES_LAYER = 2 * TB * WAVES
        staged = sem("staged", WAVES_LAYER)
        gathered = [sem(f"gathered{q}", 16 * QUAD * WAVES_LAYER) for q in range(QUADS)]
        quad_free = sem("quad_free", QUADS * WAVES_LAYER)
        gelu_done = sem("gelu_done", TB)
        wgt_ready = sem("wgt_ready", TB)
        diag_ready = sem("diag_ready", TB * 3 * QUADS * WAVES)
        diag_used = sem("diag_used", 2 + TB * 3 * QUADS * WAVES)
        dve_step = sem("dve_step", DVE_STEPS)
        out_ready = once("out_ready")
        fin_step = once("fin_step")
        fin_act = once("fin_act")
        stored = once("stored")

        block = ctx.enter_context(nc.Block())

        @block.sync
        def _(sync):
            sync.dma_start(cst[:], consts).then_inc(setup_loaded, 16)
            sync.dma_start(x_tok[:], x[0].rearrange("(b p) d -> p b d", p=P)).then_inc(setup_loaded, 16)
            sync.dma_start(par_all[:], params.rearrange("l p n -> p l n")).then_inc(setup_loaded, 16)
            sync.dma_start(pos_i[:], positions.broadcast_to([P, SEQ])).then_inc(setup_loaded, 16)
            sync.dma_start(wdt_all[:], w_dt.rearrange("l p n -> p l n")).then_inc(setup_loaded, 16)
            for s in range(2):
                sync.dma_start(w_ring[:, s, :], w_stream[s]).then_inc(chunk_loaded[s].sem, 16)
            with sync.Fori(0, DEPTH * CHUNKS // 2 - 1) as i:
                for s in range(2):
                    sync.wait_ge(chunk_begun.sem, 2 * i + s + 2)
                    sync.dma_start(w_ring[:, s, :], w_stream[bass.ds(2 * i + s + 2, 1)].rearrange("a p n -> p (a n)"))\
                        .then_inc(chunk_loaded[s].sem, 16)
            sync.wait_ge(out_ready, 1)
            sync.dma_start(out[0].rearrange("(b p) d -> p b d", p=P), h2[:]).then_inc(stored, 16)
            sync.wait_ge(stored, 16)

        @block.tensor
        def _(pe):
            def wait(sig, n, L):
                pe.wait_ge(sig.sem, sig.at(L, n))

            def wait_alone(sig, value):
                value = pe.to_reg(value)
                pe.wait_ge(setup_loaded, 80)
                pe.wait_ge(sig.sem, value)

            pe.wait_ge(setup_loaded, 80)
            with pe.Fori(0, DEPTH) as L:

                def chunk_wait(c):
                    wait(chunk_loaded[c % 2], 16 * (c // 2 + 1), L)

                def turn_normed(u):
                    wait(xn_ready, u + 1, L)
                    for j in range(4):
                        for k in (2 * j, 2 * j + 1):
                            for b in range(TB):
                                ins = pe.transpose(two(j)[:, k % 2, b * P:(b + 1) * P],
                                                   xn[:, b, k * P:(k + 1) * P], ident)
                        ins.then_inc(bank_full.sem, 1)

                def project(chunk_in_ring, rhs, b0, free, full, ks=KD, tiles=4):
                    w = w_ring[:, chunk_in_ring, :].rearrange("p (k n) -> p k n", k=ks)
                    for j in range(tiles):
                        if j % 2 == 0:
                            free(j // 2)
                        for k in range(ks):
                            ins = pe.matmul(two(b0 + j // 2)[:, j % 2, :], w[:, k, j * P:(j + 1) * P],
                                            rhs(k), start=(k == 0), stop=(k == ks - 1))
                            if j == 0 and k == 0:
                                ins.then_inc(chunk_begun.sem, 1)
                        if j % 2 == 1:
                            ins.then_inc(full.sem, 1)

                turn_normed(0)
                wait_alone(bank_empty, bank_empty.at(L, 4))
                rhs_h = lambda k: hT[:, k, :]

                def in_project(lo, hi):
                    with pe.Fori(lo, hi) as i:
                        for s in range(2):
                            pe.wait_ge(chunk_loaded[s].sem, chunk_loaded[s].at(L, 16 * (i + 1)))
                            project(s, rhs_h, 2 * s,
                                    lambda q: pe.wait_ge(bank_empty.sem, bank_empty.at(L, 4 * i + 2 * s + q + 1)),
                                    bank_full)

                in_project(0, 4)
                for b in range(TB):
                    for k in range(KD):
                        ins = pe.matmul(bank[4][:, b * 2 * SH:(b + 1) * 2 * SH], hT[:, k, b * P:(b + 1) * P],
                                        wdt_all[:, bass.ds(L, 1), k * 2 * SH:(k + 1) * 2 * SH], start=(k == 0), stop=(k == KD - 1))
                ins.then_inc(dt_proj.sem, 1)
                in_project(4, 8)
                for h in range(HEADS):
                    if h == 0:
                        wait(bank_empty, 4 + 24, L)
                        wait(dt_abs_in, 1, L)
                    if h >= 4:
                        wait(rot_empty, h - 3, L)
                    pe.matmul(bank[4 + h % 4][:], const("prot"), qk[:, 2 * h:2 * h + 2, :], start=True, stop=True)\
                        .then_inc(rot_full.sem, 1)
                in_project(8, 10)
                for c in range(2):
                    chunk_wait(C_V + c)
                    w = w_ring[:, c, :].rearrange("p (k n) -> p k n", k=KD)
                    for b in range(TB):
                        m = 44 + 2 * c + b
                        wait(bank_empty, m - 3, L)
                        for k in range(KD):
                            ins = pe.matmul(bank[m % 4][:], hT[:, k, b * P:(b + 1) * P], w[:, k, :],
                                            start=(k == 0), stop=(k == KD - 1))
                            if b == 0 and k == 0:
                                ins.then_inc(chunk_begun.sem, 1)
                        ins.then_inc(bank_full.sem, 1)
                wait(a_ready, 1, L)
                wait(rot_empty, HEADS, L)
                for b in range(TB):
                    pe.matmul(bank[7][:, b * 64:b * 64 + SH], tri_le, a_v[:, b, 0:SH], start=True, stop=True)
                    pe.matmul(bank[7][:, b * 64 + SH:(b + 1) * 64], tri_ge, a_v[:, b, SH:2 * SH], start=True, stop=True)
                    ins = pe.matmul(bank[7][:, 128 + b * 64:128 + (b + 1) * 64], ones, a_v[:, b, :],
                                    start=True, stop=True)
                ins.then_inc(cums_done.sem, 1)
                wait(cums_copied, 1, L)

                def scores(h):
                    p = h % 2
                    if h == 0:
                        wait(bank_empty, 48, L)
                    if h >= 2:
                        wait(exp_done, h - 1, L)
                    for c in range(2):
                        for b in range(TB):
                            ins = pe.matmul(two(2 * p + c)[:, b, :], qk[c * HD:(c + 1) * HD, h, b * P:(b + 1) * P],
                                            qk[c * HD:(c + 1) * HD, HEADS + h, :], start=True, stop=True)
                    ins.then_inc(sc_done.sem, 1)

                scores(0)
                for h in range(HEADS):
                    p = h % 2
                    if h + 1 < HEADS:
                        scores(h + 1)
                    wait(w_ready, h + 1, L)
                    if h >= 2:
                        wait(wT_ready, h - 1, L)
                    for kb in range(TB):
                        for b in range(TB):
                            ins = pe.transpose(two(4 + p)[:, kb, b * P:(b + 1) * P],
                                               e_buf[:, p, 0, b, kb * P:(kb + 1) * P], ident)
                    ins.then_inc(w_turned.sem, 1)
                    wait(wT_ready, h + 1, L)
                    if h >= 2:
                        wait(o_copied, h - 1, L)
                    for b in range(TB):
                        for kb in range(TB):
                            ins = pe.matmul(bank[6 + p][:, b * VD:(b + 1) * VD], wT[:, p, kb, b * P:(b + 1) * P],
                                            v_tok[:, kb, h * VD:(h + 1) * VD], start=(kb == 0), stop=(kb == TB - 1))
                    ins.then_inc(av_done.sem, 1)
                wait(att_normed, 1, L)
                for j in range(4):
                    for h in (2 * j, 2 * j + 1):
                        for b in range(TB):
                            ins = pe.transpose(two(j)[:, h % 2, b * P:(b + 1) * P], o_view[:, b, h, :], ident)
                    ins.then_inc(bank_full.sem, 1)
                wait(bank_empty, 52, L)
                for c in range(2):
                    chunk_wait(C_ATT + c)
                    project(c % 2, lambda k: attT[:, k, :], 2 * c, lambda q: None, mix_full)

                for i in range(8):
                    b, c = divmod(i, 4)
                    if i == 0:
                        wait(xbc_ready, NXBC // 2, L)
                    if i < 4:
                        wait(mix_empty, i + 1, L)
                    else:
                        wait(xt_empty, i - 3, L)
                    for j in range(4):
                        ins = pe.transpose(bank[i % 4][:, j * P:(j + 1) * P], xbc[:, 4 * c + j, b * P:(b + 1) * P], ident)
                    ins.then_inc(xt_full.sem, 1)

                def decays(g):
                    for t in range(4):
                        wait(atri_ready, 4 * g + t + 1, L)
                        if g == 0:
                            if t == 0:
                                wait(xt_empty, 8, L)
                        else:
                            wait(diff_ready, 4 * (g - 1) + t + 1, L)
                            if t == 1:
                                wait(offexp_done, 2 * g - 1, L)
                            if t == 2:
                                wait(offexp_done, 2 * g, L)
                        pe.matmul(bank[t][:], ones, a_tri[:, t, :, :], start=True, stop=True)\
                            .then_inc(f_done.sem, 1)
                    if g == 0:
                        wait(wT_ready, HEADS, L)
                    else:
                        wait(cb_masked, g, L)
                        wait(cboff_copied, g, L)
                    for s in range(TB):
                        ins = pe.matmul(two(4)[:, s, :], xbc[:, XT + g, s * P:(s + 1) * P], xbc[:, XT + GROUPS + g, :],
                                        start=True, stop=True)
                    ins.then_inc(cb_done.sem, 1)

                decays(0)
                for g in range(GROUPS):
                    p = g % 2
                    if g + 1 < GROUPS:
                        decays(g + 1)
                    wait(m_ready, g + 1, L)
                    if g == 0:
                        wait(o_copied, HEADS, L)
                    if g >= 2:
                        wait(y_copied, g - 1, L)
                    for l in range(TB):
                        terms = [(0, 0, x_fwd), (2, 0, x_bwd), (5, 1, x_bwd)] if l == 0 else \
                                [(1, 1, x_fwd), (3, 1, x_bwd), (4, 0, x_fwd)]
                        for r in range(HPG):
                            h = HPG * g + r
                            col = l * HPG * SP_ + r * SP_
                            for n, (t, s, xs) in enumerate(terms):
                                ins = pe.matmul(bank[5 + p][:, col:col + SP_], m_mat[:, p, t, r, :],
                                                xs[:, s, h * SP_:(h + 1) * SP_], start=(n == 0), stop=(n == 2))
                    ins.then_inc(y_done.sem, 1)
                    wait(y_copied, g + 1, L)
                    if g >= 1:
                        wait(yz_ready, g, L)
                    for j in range(2):
                        for l in range(TB):
                            ins = pe.transpose(two(7)[:, j, l * P:(l + 1) * P], y_grp[:, p, l, j * P:(j + 1) * P], ident)
                    ins.then_inc(y_turned.sem, 1)
                for i in range(XT // 2):
                    wait(ysq_ready, i + 1, L)
                    for u in range(2):
                        ins = pe.matmul(bank[4][:, 0:SEQ], ones, y_sq2[:, i % 2, u, :],
                                        start=(i == 0 and u == 0), stop=(i == XT // 2 - 1 and u == 1))
                    ins.then_inc(ysq_used.sem, 1)
                wait(m_scaled, 1, L)
                for c in range(4):
                    chunk_wait(C_SSM + c)
                    project(c % 2, lambda k: zT[:, k, :], c, lambda q: None, mix_full, ks=XT, tiles=2)
                wait(mix_empty, 8, L)
                for c in range(2):
                    chunk_wait(C_OUT + c)
                    w = w_ring[:, c, :].rearrange("p (k n) -> p k n", k=KD)
                    for b in range(TB):
                        for k in range(KD):
                            ins = pe.matmul(bank[2 * c + b][:], gateT[:, k, b * P:(b + 1) * P], w[:, k, :],
                                            start=(k == 0), stop=(k == KD - 1))
                            if b == 0 and k == 0:
                                ins.then_inc(chunk_begun.sem, 1)
                        ins.then_inc(mix_full.sem, 1)

                turn_normed(1)
                wait(bank_empty, 56, L)
                for c in range(4):
                    chunk_wait(C_WQ + c)
                    m = 56 + 2 * c
                    project(c % 2, rhs_h, 2 * (c % 2), lambda q: wait(bank_empty, m + q - 3, L), bank_full)
                wait(peer_loaded, 32, L)
                for i in range(8):
                    b, c = divmod(i, 4)
                    m = 64 + i
                    wait(bank_empty, 64 if i == 0 else m - 3, L)
                    for j in range(4):
                        t = 4 * c + j
                        ins = pe.matmul(bank[m % 4][:, j * PK:(j + 1) * PK], qryT[:, t, b * P:(b + 1) * P], keys[:, t, :],
                                        start=True, stop=True)
                    ins.then_inc(bank_full.sem, 1)

                for b in range(TB):
                    b0 = 4 + 2 * b
                    if b == 0:
                        wait(bank_empty, STREAM, L)
                    for n in range(2):
                        ins = pe.matmul(bank[b0 + n][:], ident, x_tok[:, b, n * 512:(n + 1) * 512], start=True,
                                        stop=False, skip_group_check=True)
                        if b == 0:
                            ins.then_inc(diag_used.sem, 1)
                    with pe.Fori(0, WAVES) as w:
                        for q in range(QUADS):
                            pe.wait_ge(gathered[q].sem,
                                       gathered[q].at(L, 16 * QUAD * (WAVES * (2 * b + 1) + w + 1)))
                            for s in range(3):
                                pe.wait_ge(diag_ready.sem, diag_ready.at(L, 3 * (QUADS * (WAVES * b + w) + q) + s + 1))
                                for n in range(2):
                                    ins = pe.matmul(bank[b0 + n][:], diag[:, s, :],
                                                    ring[:, QUAD * q + s, n * 512:(n + 1) * 512],
                                                    start=False, stop=True, skip_group_check=True)
                                ins.then_inc(diag_used.sem, 1)

        @block.scalar
        def _(act):
            def wait(sig, n, L):
                act.wait_ge(sig.sem, sig.at(L, n))

            def wait_alone(sig, value):
                value = act.to_reg(value)
                act.wait_ge(setup_loaded, 80)
                act.wait_ge(sig.sem, value)

            def squares(u, L):
                for b in range(TB):
                    ins = act.activation(xn[:, b, :], x_tok[:, b, :], ACT.Square, accum_out=ssq[:, b:b + 1])
                ins.then_inc(sq_done.sem, 1)
                wait(ms_ready, u + 1, L)
                act.activation(rms[:], rms[:], ACT.Sqrt).then_inc(rms_ready.sem, 1)

            def gained(m0, gain, L):
                for j in range(4):
                    wait(bank_full, m0 + j + 1, L)
                    for k in (2 * j, 2 * j + 1):
                        ins = act.activation(hT[:, k, :], two(j)[:, k % 2, :], ACT.Copy, scale=param(gain, k, 1))
                    ins.then_inc(bank_empty.sem, 1)

            act.wait_ge(setup_loaded, 80)
            act.wait_ge(trig_ready, 1)
            act.activation(sin_t[:], trig[:, 2, :], ACT.Sin)
            act.activation(cos_t[:], trig[:, 3, :], ACT.Sin).then_inc(tables_ready, 1)

            act.wait_ge(tables_ready, 1)

            with act.Fori(0, DEPTH) as L:
                wait(x_ready, 1, L)
                squares(0, L)
                wait(par_ready, 1, L)
                act.activation(aneg[:], param("alog"), ACT.Exp).then_inc(alog_exp.sem, 1)
                gained(0, "n1g", L)
                with act.Fori(0, NXBC // 8) as i:
                    for q in range(4):
                        wait_alone(bank_full, bank_full.at(L, 4 + 4 * i + q + 1))
                        act.activation(xbc[:, bass.ds(8 * i + 2 * q, 2), :], two(q), ACT.Copy).then_inc(bank_empty.sem, 1)
                        wait_alone(conv_taps, conv_taps.at(L, CONV * (4 * i + q + 1)))
                        act.activation(xbc[:, bass.ds(8 * i + 2 * q, 2), :], c_tmp[:, q % 2], ACT.Silu)\
                            .then_inc(xbc_ready.sem, 1)
                for i in range(8):
                    wait(bank_full, 20 + i + 1, L)
                    act.activation(qk[:, 2 * i:2 * i + 2, :], two(i % 4), ACT.Copy).then_inc(bank_empty.sem, 1)
                for i in range(8):
                    wait(bank_full, 28 + i + 1, L)
                    act.activation(zT[:, 2 * i:2 * i + 2, :], two(i % 4), ACT.Silu).then_inc(bank_empty.sem, 1)
                wait(dt_abs_in, 1, L)
                act.activation(sp[:, 1, :], sp[:, 0, :], ACT.Abs).then_inc(dt_act.sem, 1)
                wait(dt_act, 1, L)
                act.activation(sp[:, 1, :], sp[:, 1, :], ACT.Exp, scale=-1.0).then_inc(dt_act.sem, 1)
                wait(lam_in, 1, L)
                act.activation(lam2[:], lam2[:], ACT.Exp).then_inc(lam_exp.sem, 1)
                for i in range(8):
                    wait(bank_full, 36 + i + 1, L)
                    for j in range(2):
                        ins = act.activation(gateT[:, 2 * i + j, :], two(i % 4)[:, j, :], ACT.Sigmoid,
                                             bias=param("gb", 2 * i + j, 1))
                    ins.then_inc(bank_empty.sem, 1)
                for i in range(4):
                    c, b = divmod(i, 2)
                    wait(bank_full, 44 + i + 1, L)
                    act.activation(v_tok[:, b, c * 512:(c + 1) * 512], bank[i][:], ACT.Copy).then_inc(bank_empty.sem, 1)

                def exps(h):
                    p = h % 2
                    wait(nb_ready, h + 1, L)
                    if h >= 2:
                        wait(w_turned, h - 1, L)
                    for c in range(2):
                        for b in range(TB):
                            ins = act.activation(e_buf[:, p, c, b, :], two(2 * p + c)[:, b, :], ACT.Exp,
                                                 bias=nb[:, p, c, b:b + 1], scale=HD ** -0.5,
                                                 accum_out=sums[:, p, c, b:b + 1])
                    ins.then_inc(exp_done.sem, 1)

                exps(0)
                for h in range(HEADS):
                    p = h % 2
                    if h + 1 < HEADS:
                        exps(h + 1)
                    wait(w_turned, h + 1, L)
                    if h >= 2:
                        wait(av_done, h - 1, L)
                    act.activation(wT[:, p], two(4 + p), ACT.Copy).then_inc(wT_ready.sem, 1)
                wait(oms_ready, 1, L)
                act.activation(ossq[:], ossq[:], ACT.Sqrt).then_inc(orms_ready.sem, 1)
                for j in range(4):
                    wait(bank_full, 48 + j + 1, L)
                    act.activation(attT[:, 2 * j:2 * j + 2, :], two(j), ACT.Copy, scale=subg[:, 0:1])\
                        .then_inc(bank_empty.sem, 1)

                def copy_y(g):
                    wait(y_done, g + 1, L)
                    if g >= 2:
                        wait(y_turned, g - 1, L)
                    act.activation(y_grp[:, g % 2], bank[5 + g % 2][:].rearrange("p (l n) -> p l n", l=TB), ACT.Copy)\
                        .then_inc(y_copied.sem, 1)

                for g in range(GROUPS):
                    p = g % 2
                    if g >= 2:
                        wait(y_done, g - 1, L)
                    for t, src, col in ((4, 1, HPG * g), (5, 2, SH + HPG * g)):
                        wait(diff_ready, 4 * g + src + 1, L)
                        for r in range(HPG):
                            ins = act.activation(m_mat[:, p, t, r, :], bank[src][:, r * P:(r + 1) * P], ACT.Exp,
                                                 bias=off_b[:, col + r:col + r + 1])
                        ins.then_inc(offexp_done.sem, 1)
                    wait(cb_masked, g + 1, L)
                    if g >= 2:
                        wait(m_ready, g - 1, L)
                    act.activation(cbm[:, p, 4:6, :], bank[4][:, P:3 * P].rearrange("p (t l) -> p t l", t=2), ACT.Copy)\
                        .then_inc(cboff_copied.sem, 1)
                    for t in range(4):
                        wait(diff_ready, 4 * g + t + 1, L)
                        act.activation(m_mat[:, p, t], m_mat[:, p, t], ACT.Exp).then_inc(dec_exp.sem, 1)
                    if g >= 1:
                        copy_y(g - 1)
                copy_y(GROUPS - 1)
                for i in range(XT // 2):
                    wait(yz_ready, min(GROUPS, i + 1), L)
                    if i >= 2:
                        wait(ysq_used, i - 1, L)
                    act.activation(y_sq2[:, i % 2], zT[:, 2 * i:2 * i + 2, :], ACT.Square).then_inc(ysq_ready.sem, 1)
                wait(yms_ready, 1, L)
                act.activation(r_bc[:], r_bc[:], ACT.Sqrt).then_inc(yrms_ready.sem, 1)

                wait(mix_empty, 12, L)
                act.dma_start(keys[:], keys_t[bass.ds(L, 1)].rearrange("a p (t k) -> p (a t) k", k=PK))\
                    .then_inc(peer_loaded.sem, 16)
                act.dma_start(g2row[:], norm2_rows[bass.ds(L, 1)].broadcast_to([P, DM])).then_inc(peer_loaded.sem, 16)
                squares(1, L)
                gained(52, "n2g", L)
                wait(h2_ready, 1, L)
                for i in range(8):
                    wait(bank_full, 56 + i + 1, L)
                    act.activation(qryT[:, 2 * i:2 * i + 2, :], two(i % 4), ACT.Copy).then_inc(bank_empty.sem, 1)
                for i in range(8):
                    b, c = divmod(i, 4)
                    wait(bank_full, 64 + i + 1, L)
                    act.activation(sc[:, b, 4 * c:4 * c + 4, :], bank[i % 4][:].rearrange("p (t k) -> p t k", k=PK), ACT.Copy)\
                        .then_inc(bank_empty.sem, 1)
                for b in range(TB):
                    wait(best_shift, b + 1, L)
                    act.activation(gate_w[:, b], gate_w[:, b], ACT.Exp).then_inc(best_exp.sem, 1)

                for b in range(TB):
                    wait(quad_free, QUADS * WAVES * (2 * b + 1), L)
                    act.activation(gel[:, b, :], act_u[:, b, :], ACT.Gelu).then_inc(gelu_done.sem, 1)
                    wait(wgt_ready, b + 1, L)
                    with act.Fori(0, WAVES) as w:
                        for q in range(QUADS):
                            for s in range(3):
                                n = 3 * (QUADS * (WAVES * b + w) + q) + s
                                wait_alone(diag_used, diag_used.at(L, n + 1))
                                act.activation(diag[:, s, :], ident, ACT.Copy,
                                               scale=wgt[:, b, bass.ds(RING * w + QUAD * q + s, 1)])\
                                    .then_inc(diag_ready.sem, 1)

            wait(x_ready, 1, DEPTH)
            act.dma_start(g2row[:], final_row.broadcast_to([P, DM])).then_inc(peer_loaded.sem, 16)
            squares(0, DEPTH)

        @block.vector
        def _(dve):
            def wait(sig, n, L):
                dve.wait_ge(sig.sem, sig.at(L, n))

            def wait_alone(sig, value):
                value = dve.to_reg(value)
                dve.wait_ge(setup_loaded, 80)
                dve.wait_ge(sig.sem, value)

            dve.wait_ge(setup_loaded, 80)
            done = [0]

            def trig_do(ins):
                done[0] += 1
                ins.then_inc(trig_step, 1)
                dve.wait_ge(trig_step, done[0])

            MAGIC = 1.5 * 2.0 ** 23
            T1 = 6.28125
            T2 = math.floor((2 * math.pi - T1) * 2 ** 20) / 2 ** 20
            T3 = 2 * math.pi - T1 - T2
            trig_do(dve.tensor_copy(trig[:, 0, :], pos_i[:]))
            trig_do(dve.tensor_scalar(trig[:, 0, :], trig[:, 0, :], const("freq"), None, ALU.mult))
            for side, quarter in ((2, 0.0), (3, 0.25)):
                trig_do(dve.tensor_scalar(trig[:, 1, :], trig[:, 0, :], 1.0 / (2 * math.pi), quarter, ALU.mult, ALU.add))
                trig_do(dve.tensor_scalar(trig[:, 1, :], trig[:, 1, :], MAGIC, None, ALU.add))
                trig_do(dve.tensor_scalar(trig[:, 1, :], trig[:, 1, :], -MAGIC, None, ALU.add))
                for n, t in enumerate((T1, T2, T3)):
                    trig_do(dve.scalar_tensor_tensor(out=trig[:, side, :], in0=trig[:, 1, :], scalar=-t,
                                                     in1=trig[:, 0 if n == 0 else side, :], op0=ALU.mult, op1=ALU.add))
                if quarter:
                    trig_do(dve.tensor_scalar(trig[:, side, :], trig[:, side, :], math.pi / 2, None, ALU.add))
                trig_do(dve.tensor_scalar(trig[:, side, :], trig[:, side, :], 3.1415925, -3.1415925, ALU.min, ALU.max))
            dve.nop().then_inc(trig_ready, 1)
            dve.nop().then_inc(x_ready.sem, 1)

            with dve.Fori(0, DEPTH) as L:
                st = Steps(dve, dve_step, L)

                def step(ins):
                    st.do(ins)
                    st.wait()

                def step_alone(ins):
                    st.do(ins)
                    wait_alone(dve_step, dve_step.at(L, st.n))

                def normed(u):
                    wait(sq_done, u + 1, L)
                    dve.tensor_scalar(rms[:], ssq[:], 1.0 / DM, EPS, ALU.mult, ALU.add).then_inc(ms_ready.sem, 1)
                    wait(rms_ready, u + 1, L)
                    step(dve.reciprocal(rstd[:], rms[:]))
                    for b in range(TB):
                        ins = dve.tensor_scalar(xn[:, b, :], x_tok[:, b, :], rstd[:, b:b + 1], None, ALU.mult)
                    ins.then_inc(xn_ready.sem, 1)

                wait(x_ready, 1, L)
                dve.tensor_copy(par[:], par_all[:, bass.ds(L, 1), :].rearrange("p a n -> p (a n)"))\
                    .then_inc(par_ready.sem, 1)
                wait(par_ready, 1, L)
                lam4 = param("lam").rearrange("p (n c d) -> p n c d", n=2, c=2)
                step(dve.tensor_tensor(lamp[:], lam4[:, :, 0, :], lam4[:, :, 1, :], ALU.mult))
                dve.tensor_reduce(lam2[:], lamp[:], AX.X, ALU.add).then_inc(lam_in.sem, 1)
                step(dve.tensor_scalar(subg[:], param("laminit"), -1.0, 1.0, ALU.mult, ALU.add))
                step(dve.tensor_tensor(subg[:], subg[:], param("sub"), ALU.mult))
                normed(0)
                wait(alog_exp, 1, L)
                step_alone(dve.tensor_scalar(aneg[:], aneg[:], -1.0, None, ALU.mult))

                with dve.Fori(0, NXBC // 4) as i:
                    for u in range(2):
                        j = 2 * i + u
                        wait_alone(bank_empty, bank_empty.at(L, 4 + j + 1))
                        for n, tap in enumerate((2, 0, 1, 3, 4)):
                            lo, hi = max(0, 2 - tap), SEQ - max(0, tap - 2)
                            for v in range(2):
                                tile = 4 * i + 2 * u + v
                                src = xbc[:, bass.ds(tile, 1), lo + tap - 2:hi + tap - 2]
                                dst = c_tmp[:, u, v:v + 1, lo:hi]
                                w = par[:, bass.ds(PARAM["cw"][0] + CONV * tile + tap, 1)]
                                if n == 0:
                                    ins = dve.tensor_scalar(dst, src, w, par[:, bass.ds(PARAM["cb"][0] + tile, 1)],
                                                            ALU.mult, ALU.add)
                                else:
                                    ins = dve.scalar_tensor_tensor(out=dst, in0=src, scalar=w, in1=dst,
                                                                   op0=ALU.mult, op1=ALU.add)
                            ins.then_inc(conv_taps.sem, 1)
                            if n < CONV - 1:
                                dve.wait_ge(conv_taps.sem, conv_taps.at(L, CONV * j + n + 1))

                wait(dt_proj, 1, L)
                dve.tensor_tensor(sp[:, 0, :].rearrange("p (b n) -> p b n", b=TB),
                                  bank[4][:, 0:2 * 2 * SH].rearrange("p (b n) -> p b n", b=TB),
                                  bc(param("dtb"), 1, TB), ALU.add).then_inc(dt_abs_in.sem, 1)
                wait(dt_act, 2, L)
                step(dve.tensor_scalar(sp[:, 2, :], sp[:, 1, :], 2.0, None, ALU.add))
                step(dve.reciprocal(sp[:, 2, :], sp[:, 2, :]))
                step(dve.tensor_tensor(sp[:, 1, :], sp[:, 1, :], sp[:, 2, :], ALU.mult))
                step(dve.tensor_tensor(sp[:, 3, :], sp[:, 1, :], sp[:, 1, :], ALU.mult))
                step(dve.tensor_scalar(sp[:, 4, :], sp[:, 3, :], LOG_TERMS[0], None, ALU.mult))
                for c in LOG_TERMS[1:]:
                    step(dve.scalar_tensor_tensor(out=sp[:, 4, :], in0=sp[:, 4, :], scalar=c, in1=sp[:, 3, :],
                                                  op0=ALU.add, op1=ALU.mult))
                step(dve.scalar_tensor_tensor(out=sp[:, 4, :], in0=sp[:, 4, :], scalar=1.0, in1=sp[:, 1, :],
                                              op0=ALU.add, op1=ALU.mult))
                step(dve.tensor_scalar(sp[:, 5, :], sp[:, 0, :], 0.0, None, ALU.max))
                step(dve.scalar_tensor_tensor(out=dt_v[:].rearrange("p b n -> p (b n)"), in0=sp[:, 4, :], scalar=2.0,
                                              in1=sp[:, 5, :], op0=ALU.mult, op1=ALU.add))
                dve.tensor_tensor(a_v[:], dt_v[:], bc(aneg[:], 1, TB), ALU.mult).then_inc(a_ready.sem, 1)

                dve.wait_ge(tables_ready, 1)
                for i in range(HEADS):
                    wait(rot_full, i + 1, L)
                    if i >= 1:
                        wait(rot_empty, i, L)
                    pair = qk[:, 2 * i:2 * i + 2, :]
                    dve.tensor_tensor(rot_tmp[:], two(4 + i % 4), bc(sin_t[:], 1, 2), ALU.mult)
                    step(dve.tensor_tensor(pair, pair, bc(cos_t[:], 1, 2), ALU.mult))
                    dve.tensor_tensor(pair, pair, rot_tmp[:], ALU.add).then_inc(rot_empty.sem, 1)
                wait(cums_done, 1, L)
                step(dve.tensor_copy(f_col[:].rearrange("p b n -> p (b n)"), bank[7][:, 0:128]))
                dve.tensor_tensor(off_b[:, 0:SH], bank[7][:, 128:128 + SH], f_col[:, 0, 0:SH], ALU.subtract)
                dve.tensor_tensor(off_b[:, SH:2 * SH], bank[7][:, 192 + SH:192 + 2 * SH], f_col[:, 1, SH:2 * SH],
                                  ALU.subtract).then_inc(cums_copied.sem, 1)
                wait(lam_exp, 1, L)
                step(dve.tensor_tensor(neglam[:], lam2[:, 1:2], lam2[:, 0:1], ALU.subtract))
                step(dve.tensor_tensor(neglam[:], neglam[:], param("laminit"), ALU.subtract))

                def maxima(h):
                    p = h % 2
                    wait(sc_done, h + 1, L)
                    for c in range(2):
                        ins = dve.tensor_reduce(mx[:, p, c, :], two(2 * p + c), AX.X, ALU.max)
                    step(ins)
                    dve.tensor_scalar(nb[:, p], mx[:, p], -HD ** -0.5, None, ALU.mult).then_inc(nb_ready.sem, 1)

                def copy_o(h):
                    wait(av_done, h + 1, L)
                    dve.tensor_copy(o_view[:, :, h, :], bank[6 + h % 2][:, 0:TB * VD].rearrange("p (b e) -> p b e", b=TB))\
                        .then_inc(o_copied.sem, 1)

                maxima(0)
                for h in range(HEADS):
                    p = h % 2
                    if h + 1 < HEADS:
                        maxima(h + 1)
                    wait(exp_done, h + 1, L)
                    step(dve.reciprocal(rec[:, p], sums[:, p]))
                    step(dve.tensor_scalar(rec[:, p, 1, :], rec[:, p, 1, :], neglam[:, 0:1], None, ALU.mult))
                    for b in range(TB):
                        ins = dve.tensor_scalar(e_buf[:, p, 0, b, :], e_buf[:, p, 0, b, :], rec[:, p, 0, b:b + 1], None,
                                                ALU.mult)
                    step(ins)
                    for b in range(TB):
                        ins = dve.scalar_tensor_tensor(out=e_buf[:, p, 0, b, :], in0=e_buf[:, p, 1, b, :],
                                                       scalar=rec[:, p, 1, b:b + 1], in1=e_buf[:, p, 0, b, :],
                                                       op0=ALU.mult, op1=ALU.add)
                    ins.then_inc(w_ready.sem, 1)
                    if h >= 1:
                        copy_o(h - 1)
                copy_o(HEADS - 1)
                wait(o_copied, HEADS, L)
                o16 = o_view.rearrange("p b h e -> p (b h) e")
                step(dve.tensor_tensor(o_sq[:], o16, o16, ALU.mult))
                step(dve.tensor_reduce(ossq[:], o_sq[:], AX.X, ALU.add))
                dve.tensor_scalar(ossq[:], ossq[:], 1.0 / VD, EPS, ALU.mult, ALU.add).then_inc(oms_ready.sem, 1)
                wait(orms_ready, 1, L)
                step(dve.reciprocal(ossq[:], ossq[:]))
                dve.tensor_tensor(o16, o16, bc(ossq[:], 2, VD), ALU.mult).then_inc(att_normed.sem, 1)
                for i in range(4):
                    wait(mix_full, i + 1, L)
                    g = gateT[:, 2 * i:2 * i + 2, :]
                    dve.tensor_tensor(g, two(i), g, ALU.mult).then_inc(mix_empty.sem, 1)

                for i in range(8):
                    b, c = divmod(i, 4)
                    wait(xt_full, i + 1, L)
                    for d, xs in enumerate((x_fwd, x_bwd)):
                        ins = dve.tensor_tensor(xs[:, b, c * 512:(c + 1) * 512].rearrange("p (h n) -> p h n", n=SP_),
                                                bank[i % 4][:].rearrange("p (h n) -> p h n", n=SP_),
                                                bc(dt_v[:, b, d * SH + 8 * c:d * SH + 8 * c + 8], 2, SP_), ALU.mult)
                    ins.then_inc(xt_empty.sem, 1)

                blocks = bank[4][:].rearrange("p (a l) -> p a l", l=P)

                def differences(g):
                    p = g % 2
                    if g >= 2:
                        wait(y_done, g - 1, L)
                    for t in range(4):
                        d, b = divmod(t, 2)
                        wait(f_done, 4 * g + t + 1, L)
                        for r in range(HPG):
                            col = d * SH + HPG * g + r
                            ins = dve.tensor_scalar(m_mat[:, p, t, r, :], bank[t][:, r * P:(r + 1) * P],
                                                    f_col[:, b, col:col + 1], 0.0, ALU.subtract, ALU.min)
                        ins.then_inc(diff_ready.sem, 1)
                    wait(cb_done, g + 1, L)
                    dve.tensor_tensor(cbm[:, p, 0:2, :], blocks[:, 0:4:3, :], bc(tri_le, 1, 2), ALU.mult)
                    dve.tensor_tensor(cbm[:, p, 2:4, :], blocks[:, 0:4:3, :], bc(tri_ge, 1, 2), ALU.mult)\
                        .then_inc(cb_masked.sem, 1)

                def skip_and_gate(g):
                    wait(y_turned, g + 1, L)
                    for j in range(2):
                        t = 2 * g + j
                        ins = dve.scalar_tensor_tensor(out=xbc[:, t, :], in0=xbc[:, t, :], scalar=param("dsk", t, 1),
                                                       in1=two(7)[:, j, :], op0=ALU.mult, op1=ALU.add)
                    step(ins)
                    zs = zT[:, 2 * g:2 * g + 2, :]
                    dve.tensor_tensor(zs, zs, xbc[:, 2 * g:2 * g + 2, :], ALU.mult).then_inc(yz_ready.sem, 1)

                differences(0)
                for g in range(GROUPS):
                    p = g % 2
                    if g + 1 < GROUPS:
                        differences(g + 1)
                    wait(cb_masked, g + 1, L)
                    for t in range(4):
                        wait(dec_exp, 4 * g + t + 1, L)
                        dve.tensor_tensor(m_mat[:, p, t], m_mat[:, p, t], bc(cbm[:, p, t, :], 1, HPG), ALU.mult)
                    wait(offexp_done, 2 * g + 2, L)
                    wait(cboff_copied, g + 1, L)
                    dve.tensor_tensor(m_mat[:, p, 4:6], m_mat[:, p, 4:6], bc(cbm[:, p, 4:6, :], 2, HPG), ALU.mult)\
                        .then_inc(m_ready.sem, 1)
                    if g >= 1:
                        skip_and_gate(g - 1)
                skip_and_gate(GROUPS - 1)
                wait(yz_ready, GROUPS, L)
                for t in range(XT):
                    wait(ysq_ready, t // 2 + 1, L)
                    ins = dve.tensor_scalar(zT[:, t, :], zT[:, t, :], param("sng", t, 1), None, ALU.mult)
                ins.then_inc(m_scaled.sem, 1)
                wait(ysq_used, XT // 2, L)
                dve.tensor_scalar(r_bc[:], bank[4][:, 0:SEQ], 1.0 / INNER, EPS, ALU.mult, ALU.add)\
                    .then_inc(yms_ready.sem, 1)
                wait(yrms_ready, 1, L)
                step(dve.reciprocal(r_bc[:], r_bc[:]))
                step(dve.tensor_tensor(gateT[:, KD:2 * KD, :], gateT[:, KD:2 * KD, :], bc(r_bc[:], 1, KD), ALU.mult))
                for i in range(4):
                    wait(mix_full, 4 + i + 1, L)
                    step(dve.tensor_tensor(s_tmp[:, 0:2, :], two(i), gateT[:, KD + 2 * i:KD + 2 * i + 2, :], ALU.mult))
                    g = gateT[:, 2 * i:2 * i + 2, :]
                    dve.tensor_tensor(g, g, s_tmp[:, 0:2, :], ALU.add).then_inc(mix_empty.sem, 1)
                    wait(mix_empty, 4 + i + 1, L)
                for i in range(4):
                    c, b = divmod(i, 2)
                    wait(mix_full, 8 + i + 1, L)
                    xs = x_tok[:, b, c * 512:(c + 1) * 512]
                    dve.tensor_tensor(xs, bank[i][:], xs, ALU.add).then_inc(mix_empty.sem, 1)

                normed(1)
                wait(peer_loaded, 32, L)
                wait(xn_ready, 2, L)
                dve.tensor_tensor(h2[:], xn[:], bc(g2row[:], 1, TB), ALU.mult).then_inc(h2_ready.sem, 1)

                for b in range(TB):
                    wait_alone(bank_empty, bank_empty.at(L, 64 + 4 * (b + 1)))
                    top = range(2 * PH)
                    for t in top:
                        ins = dve.max(vals[:, b, t, 0:8], sc[:, b, t, :])
                    step_alone(ins)
                    for t in top:
                        ins = dve.max_index(idxs[:, b, t, 0:8], vals[:, b, t, 0:8], sc[:, b, t, :])
                    step_alone(ins)
                    for t in top:
                        ins = dve.match_replace(sc[:, b, t, :], vals[:, b, t, 0:8], sc[:, b, t, :], NEG)
                    step_alone(ins)
                    for t in top:
                        ins = dve.max(vals[:, b, t, 8:16], sc[:, b, t, :])
                    step_alone(ins)
                    for t in top:
                        ins = dve.max_index(idxs[:, b, t, 8:16], vals[:, b, t, 8:16], sc[:, b, t, :])
                    step_alone(ins)
                    wait(bank_empty, STREAM, L)
                    v4 = vals[:, b].rearrange("p (h c) k -> p h c k", c=2)
                    step_alone(dve.tensor_tensor(cand[:], bc(v4[:, :, 0, :], 3, TOPK), bc(v4[:, :, 1, :], 2, TOPK), ALU.add))
                    flat = cand[:].rearrange("p h i j -> p h (i j)")
                    for h in range(PH):
                        ins = dve.max(best[:, b, h, 0:8], flat[:, h, :])
                    step_alone(ins)
                    for h in range(PH):
                        ins = dve.max_index(posn[:, b, h, 0:8], best[:, b, h, 0:8], flat[:, h, :])
                    step_alone(ins)
                    for h in range(PH):
                        ins = dve.match_replace(flat[:, h, :], best[:, b, h, 0:8], flat[:, h, :], NEG)
                    step_alone(ins)
                    for h in range(PH):
                        ins = dve.max(best[:, b, h, 8:16], flat[:, h, :])
                    step_alone(ins)
                    for h in range(PH):
                        ins = dve.max_index(posn[:, b, h, 8:16], best[:, b, h, 8:16], flat[:, h, :])
                    step_alone(ins)
                    pv = posn[:, b].rearrange("p h k -> p (h k)")
                    dve.tensor_scalar(ab_u[:, 0, :], pv, 4, None, ALU.logical_shift_right)
                    dve.tensor_scalar(ab_u[:, 1, :], pv, 15, None, ALU.bitwise_and)
                    step(dve.tensor_copy(idxf[:], idxs[:, b]))
                    step(dve.tensor_copy(ab_f[:], ab_u[:]))
                    i4 = idxf[:].rearrange("p (h c) k -> p h c k", c=2)
                    for c in range(2):
                        step(dve.tensor_tensor(eq[:].rearrange("p h k j -> p (h k) j"), bc(ab_f[:, c, :], 2, TOPK),
                                               bc(const("iota"), 1, SLOTS), ALU.is_equal))
                        step(dve.tensor_tensor(eq[:], eq[:], bc(i4[:, :, c, :], 2, TOPK), ALU.mult))
                        step(dve.tensor_reduce(selv[:, c, :], eq[:].rearrange("p h k j -> p (h k) j"), AX.X, ALU.add))
                    step(dve.scalar_tensor_tensor(out=selv[:, 0, :], in0=selv[:, 0, :], scalar=float(PK),
                                                  in1=selv[:, 1, :], op0=ALU.mult, op1=ALU.add))
                    dve.tensor_scalar(ex_i[:, b, :], selv[:, 0, :], param("row0"), None, ALU.add)\
                        .then_inc(experts_ready.sem, 1)
                    dve.tensor_tensor(gate_w[:, b], best[:, b], best[:, b, :, 0:1].broadcast_to([P, PH, TOPK]),
                                      ALU.subtract).then_inc(best_shift.sem, 1)
                    wait(best_exp, b + 1, L)
                    step(dve.tensor_reduce(gsum[:, b], gate_w[:, b], AX.X, ALU.add))
                    step(dve.reciprocal(gsum[:, b], gsum[:, b]))
                    step_alone(dve.tensor_tensor(gate_w[:, b], gate_w[:, b], bc(gsum[:, b], 2, TOPK), ALU.mult))

                for b in range(TB):
                    with dve.Fori(0, WAVES) as w:
                        for q in range(QUADS):
                            dve.wait_ge(gathered[q].sem, gathered[q].at(L, 16 * QUAD * (WAVES * 2 * b + w + 1)))
                            for s in range(QUAD):
                                row = ring[:, QUAD * q + s, :]
                                ins = dve.scalar_tensor_tensor(out=row, in0=row, scalar=1.0, in1=h2[:, b, :],
                                                               op0=ALU.mult, op1=ALU.mult,
                                                               accum_out=act_u[:, b, bass.ds(RING * w + QUAD * q + s, 1)])
                            ins.then_inc(quad_free.sem, 1)
                    step(dve.memset(acc_v[:], 0.0))
                    wait(gelu_done, b + 1, L)
                    dve.tensor_tensor(wgt[:, b, :], gel[:, b, :], gate_w[:, b].rearrange("p h k -> p (h k)"), ALU.mult)\
                        .then_inc(wgt_ready.sem, 1)
                    wait_alone(wgt_ready, wgt_ready.at(L, b + 1))
                    with dve.Fori(0, WAVES) as w:
                        for q in range(QUADS):
                            n = QUADS * (WAVES * (2 * b + 1) + w) + q
                            dve.wait_ge(gathered[q].sem, gathered[q].at(L, 16 * QUAD * (WAVES * (2 * b + 1) + w + 1)))
                            dve.wait_ge(quad_free.sem, quad_free.at(L, n))
                            dve.scalar_tensor_tensor(out=acc_v[:], in0=ring[:, QUAD * q + 3, :],
                                                     scalar=wgt[:, b, bass.ds(RING * w + QUAD * q + 3, 1)],
                                                     in1=acc_v[:], op0=ALU.mult, op1=ALU.add).then_inc(quad_free.sem, 1)
                    wait(quad_free, QUADS * WAVES * (2 * b + 2), L)
                    wait(diag_used, 2 + 3 * QUADS * WAVES * (b + 1), L)
                    for n in range(2):
                        ins = dve.tensor_tensor(x_tok[:, b, n * 512:(n + 1) * 512], bank[4 + 2 * b + n][:],
                                                acc_v[:, n * 512:(n + 1) * 512], ALU.add)
                    ins.then_inc(x_ready.sem, 1)
                    wait_alone(x_ready, x_ready.at(L, b + 2))
                assert st.n == DVE_STEPS, st.n

            dve.wait_ge(sq_done.sem, sq_done.at(DEPTH, 1))
            dve.tensor_scalar(rms[:], ssq[:], 1.0 / DM, EPS, ALU.mult, ALU.add).then_inc(ms_ready.sem, 1)
            dve.wait_ge(rms_ready.sem, rms_ready.at(DEPTH, 1))
            dve.reciprocal(rstd[:], rms[:]).then_inc(fin_step, 1)
            dve.wait_ge(fin_step, 1)
            dve.wait_ge(peer_loaded.sem, peer_loaded.at(DEPTH, 16))
            for b in range(TB):
                ins = dve.scalar_tensor_tensor(out=h2[:, b, :], in0=x_tok[:, b, :], scalar=rstd[:, b:b + 1], in1=g2row[:],
                                               op0=ALU.mult, op1=ALU.mult)
            ins.then_inc(out_ready, 1)

        @block.gpsimd
        def _(pool):
            def wait(sig, n, L):
                pool.wait_ge(sig.sem, sig.at(L, n))

            def wait_alone(*waits):
                waits = [(sig, pool.to_reg(value)) for sig, value in waits]
                pool.wait_ge(setup_loaded, 80)
                for sig, value in waits:
                    pool.wait_ge(sig.sem, value)

            pool.wait_ge(setup_loaded, 80)
            with pool.Fori(0, DEPTH) as L:
                wait(a_ready, 1, L)
                for g in range(GROUPS):
                    for t in range(4):
                        d, b = divmod(t, 2)
                        if g >= 1:
                            wait(f_done, 4 * (g - 1) + t + 1, L)
                        pool.tensor_tensor(a_tri[:, t], bc(tri_ge if d else tri_le, 1, HPG),
                                           bc(a_v[:, b, d * SH + HPG * g:d * SH + HPG * (g + 1)], 2, P), ALU.mult)\
                            .then_inc(atri_ready.sem, 1)

                def wave(b, table, w, half, opening):
                    n = WAVES * (2 * b + table) + w
                    pool.tensor_copy(stage[:, half, :], ex_i[:, b, bass.ds(RING * w, RING)]).then_inc(staged.sem, 1)
                    for q in range(QUADS):
                        waits = []
                        if q == 0:
                            waits.append((staged, staged.at(L, n + 1)))
                        if not (opening and b == 0 and table == 0):
                            waits.append((quad_free, quad_free.at(L, QUADS * (n - 1) + q + 1)))
                        if table == 0 and b > 0:
                            waits.append((diag_used, diag_used.at(L, 2 + 3 * QUADS * WAVES * b)))
                        if table == 1 and not opening:
                            waits.append((diag_used, diag_used.at(L, 2 + 3 * (QUADS * (WAVES * b + w - 1) + q + 1))))
                        wait_alone(*waits)
                        for s in range(QUAD):
                            r = QUAD * q + s
                            pool.indirect_dma_start(ring[:, r, :], None, peer_v if table else peer_u,
                                                    bass.IndirectOffsetOnAxis(ap=stage[:, half, r:r + 1], axis=0))\
                                .then_inc(gathered[q].sem, 16)

                for b in range(TB):
                    wait_alone((experts_ready, experts_ready.at(L, b + 1)))
                    for table in range(2):
                        wave(b, table, 0, 0, True)
                        wave(b, table, 1, 1, False)
                        with pool.Fori(1, WAVES // 2) as i:
                            wave(b, table, 2 * i, 0, False)
                            wave(b, table, 2 * i + 1, 1, False)


DVE_STEPS = 129


def _columns(w, parts):
    d, k, n = w.shape
    return w.reshape(d, k // P, P, parts, n // parts).transpose(0, 3, 2, 1, 4).reshape(d, parts, P, -1)


def _features(v):
    return v.reshape(DEPTH, -1, P).transpose(0, 2, 1)


def _rows(v):
    return np.broadcast_to(v.reshape(DEPTH, 1, -1), (DEPTH, P, v[0].size))


def _constants():
    c = np.zeros((P, NCONST), np.float32)
    col = {k: slice(*v) for k, v in CONST.items()}
    i = np.arange(P)
    c[:, col["ident"]] = np.eye(P)
    c[:, col["tri_le"]] = i[:, None] <= i[None, :]
    c[:, col["tri_ge"]] = i[:, None] >= i[None, :]
    c[:, col["ones"]] = 1.0
    half = ROPE // 2
    prot = np.zeros((P, P), np.float32)
    freq = np.zeros(P, np.float32)
    for c0 in range(0, P, HD):
        for j in range(half):
            prot[c0 + half + j, c0 + j] = -1.0
            prot[c0 + j, c0 + half + j] = 1.0
            freq[c0 + j] = freq[c0 + half + j] = np.float32(THETA ** (-2.0 * j / ROPE))
    c[:, col["prot"]] = prot
    c[:, col["iota"]] = np.arange(TOPK)
    c[:, col["freq"]] = freq[:, None]
    return c


def kernel(x, positions, norm1_g, w_in, gate_b, diff_lam, subln_g, w_att_br, conv_w, conv_b, dt_bias, a_log, d_skip,
           ssm_norm_g, w_ssm_br, w_out, norm2_g, peer_wq, peer_keys, peer_u, peer_v, final_g):
    import concourse.bacc as bacc
    from concourse.bass_utils import run_bass_kernel_spmd

    a = {k: np.asarray(v) for k, v in dict(
        x=x, positions=positions, norm1_g=norm1_g, w_in=w_in, gate_b=gate_b, diff_lam=diff_lam, subln_g=subln_g,
        w_att_br=w_att_br, conv_w=conv_w, conv_b=conv_b, dt_bias=dt_bias, a_log=a_log, d_skip=d_skip,
        ssm_norm_g=ssm_norm_g, w_ssm_br=w_ssm_br, w_out=w_out, norm2_g=norm2_g, peer_wq=peer_wq, peer_keys=peer_keys,
        peer_u=peer_u, peer_v=peer_v, final_g=final_g).items()}
    w = a["w_in"]
    q0, v0, z0, x0, d0, g0, n = 0, 2048, 3072, 5120, 9216, 9280, 11328
    w_stream = np.concatenate([
        _columns(w[:, :, x0:d0], 8), _columns(w[:, :, q0:v0], 4), _columns(w[:, :, z0:x0], 4),
        _columns(w[:, :, g0:n], 4), _columns(w[:, :, v0:z0], 2), _columns(a["w_att_br"], 2),
        _columns(a["w_ssm_br"], 4), _columns(a["w_out"], 2), _columns(a["peer_wq"], 4)], axis=1)
    conv = a["conv_w"].transpose(0, 2, 1).reshape(DEPTH, NXBC, P, CONV).transpose(0, 2, 1, 3).reshape(DEPTH, P, -1)
    skip = np.repeat(a["d_skip"], SP_, axis=1)
    lam_init = np.array([[0.8 - 0.6 * math.exp(-0.3 * l)] for l in range(DEPTH)], np.float32)
    row0 = np.array([[l * EXPERTS] for l in range(DEPTH)], np.float32)
    params = np.concatenate([
        _features(a["norm1_g"]), _features(a["norm2_g"]), _features(a["ssm_norm_g"]), conv, _features(a["conv_b"]),
        _features(a["gate_b"]), _features(a["subln_g"]), _features(skip), _rows(a["dt_bias"]), _rows(a["a_log"]),
        _rows(a["diff_lam"]), _rows(lam_init), _rows(row0)], axis=2)
    arrays = {
        "x": a["x"],
        "positions": a["positions"],
        "consts": _constants(),
        "params": params,
        "w_stream": w_stream.reshape(DEPTH * CHUNKS, P, 4096),
        "w_dt": _columns(w[:, :, d0:g0], 1)[:, 0],
        "keys_t": a["peer_keys"].reshape(DEPTH, 2 * PH, PK, P).transpose(0, 3, 1, 2).reshape(DEPTH, P, 2 * PH * PK),
        "norm2_rows": a["norm2_g"],
        "final_row": a["final_g"].reshape(1, DM),
        "peer_u": a["peer_u"].reshape(DEPTH * EXPERTS, DM),
        "peer_v": a["peer_v"].reshape(DEPTH * EXPERTS, DM),
    }
    nc = bacc.Bacc("TRN2", target_bir_lowering=False, num_devices=1)
    ins, maps = [], {}
    for name, v in arrays.items():
        v = np.ascontiguousarray(v)
        maps[f"in_{name}"] = v
        ins.append(nc.dram_tensor(f"in_{name}", v.shape, mybir.dt.from_np(v.dtype), kind="ExternalInput").ap())
    out = nc.dram_tensor("out", (1, SEQ, DM), F32, kind="ExternalOutput").ap()
    encoder_kernel(nc, *ins, out)
    r = run_bass_kernel_spmd(nc, [maps], core_ids=[0])
    return r.results[0]["out"]
```

```python
import math
from contextlib import ExitStack

import numpy as np
import concourse.bass as bass
from concourse import mybir

F32 = mybir.dt.float32
U32 = mybir.dt.uint32
I32 = mybir.dt.int32
ALU = mybir.AluOpType
ACT = mybir.ActivationFunctionType
AX = mybir.AxisListType

DEPTH, SEQ, DM = 2, 256, 1024
P = 128
TB = SEQ // P
KD = DM // P
HEADS, HD, VD = 8, 64, 128
ROPE = HD // 4
THETA = 500000.0
INNER, SH, SP_, GROUPS, STATE, CONV = 2048, 32, 64, 8, 128, 5
HPG = SH // GROUPS
XT = INNER // P
NXBC = (INNER + 2 * GROUPS * STATE) // P
PH, PK, TOPK = 8, 128, 16
EXPERTS = PK * PK
SLOTS = PH * TOPK
EPS = 1e-6
NEG = -3.0e38

C_QK, C_V, C_XBC, C_GATT, C_ATT, C_Z, C_GSSM, C_SSM, C_OUT, C_WQ, CHUNKS = 0, 4, 6, 14, 16, 18, 22, 24, 28, 30, 34
M_QK, M_V, M_XBC, M_GATT, M_ATT, M_Z, M_GSSM, M_NORM2, M_ROUTE, FILLS = 4, 12, 16, 32, 36, 40, 48, 52, 56, 72
ROUTE_FILLS = [("q", 0), ("q", 1), ("q", 2), ("s", 0, 0), ("s", 0, 1), ("q", 3), ("q", 4), ("s", 1, 0), ("s", 1, 1),
               ("q", 5), ("q", 6), ("s", 2, 0), ("s", 2, 1), ("q", 7), ("s", 3, 0), ("s", 3, 1)]

PARAM_SIZES = [("n1g", KD), ("n2g", KD), ("sng", XT), ("cw", NXBC * CONV), ("cb", NXBC), ("gb", 2 * KD),
               ("sub", 1), ("dsk", XT), ("dtb", 2 * SH), ("alog", 2 * SH), ("lam", 4 * HD), ("laminit", 1), ("row0", 1)]
PARAM = {}
FILL = {f: M_ROUTE + i for i, f in enumerate(ROUTE_FILLS)}
PARTS = PH // 2

_at = 0
for _n, _s in PARAM_SIZES:
    PARAM[_n] = (_at, _at + _s)
    _at += _s
NPAR = _at

CONST_SIZES = [("ident", P), ("tri_le", P), ("tri_ge", P), ("ones", P), ("prot", P), ("iota", TOPK), ("freq", 1)]
CONST = {}
_at = 0
for _n, _s in CONST_SIZES:
    CONST[_n] = (_at, _at + _s)
    _at += _s
NCONST = _at

RING = 16
QUAD = 4
QUADS = RING // QUAD
WAVES = SLOTS // RING

LOG_TERMS = [1.0 / (2 * k + 1) for k in range(8, 0, -1)]


class Count:

    def __init__(self, sem, per_layer):
        self.sem, self.per_layer = sem, per_layer

    def at(self, layer, n):
        return layer * self.per_layer + n


class Steps:

    def __init__(self, eng, count, layer):
        self.eng, self.count, self.layer, self.n = eng, count, layer, 0

    def do(self, ins):
        self.n += 1
        ins.then_inc(self.count.sem, 1)

    def wait(self):
        self.eng.wait_ge(self.count.sem, self.count.at(self.layer, self.n))


def bc(ap, axis, n):
    shape = list(ap.shape)
    shape.insert(axis, n)
    return ap.unsqueeze(axis).broadcast_to(shape)


def encoder_kernel(nc, x, positions, consts, params, w_stream, w_dt, keys_t, norm2_rows, final_row,
                   peer_u, peer_v, out):
    with ExitStack() as ctx:
        base = [(nc.sbuf_base + 63) // 64 * 64]
        end = nc.sbuf_usable_end

        def place(at, name, shape, dt=F32):
            size = int(np.prod(shape[1:])) * 4
            assert at + size <= end, (name, at + size, end)
            return nc.alloc_sbuf_tensor_at(name, shape, dt, offset=at), (at + size + 31) // 32 * 32

        def fixed(name, shape, dt=F32):
            t, base[0] = place(base[0], name, shape, dt)
            return t

        x_tok = fixed("x_tok", [P, TB, DM])
        hT = fixed("hT", [P, KD, SEQ])
        w_ring = fixed("w_ring", [P, 2, 4096])
        cst = fixed("cst", [P, NCONST])
        cos_t = fixed("cos_t", [P, SEQ])
        sin_t = fixed("sin_t", [P, SEQ])
        par_all = fixed("par_all", [P, DEPTH, NPAR])
        par = fixed("par", [P, NPAR])
        wdt_all = fixed("wdt_all", [P, DEPTH, KD * 2 * SH])
        ssq = fixed("ssq", [P, TB])
        rms = fixed("rms", [P, TB])
        rstd = fixed("rstd", [P, TB])
        mx = fixed("mx", [P, 2, 2, TB])
        nb = fixed("nb", [P, 2, 2, TB])
        sums = fixed("sums", [P, 2, 2, TB])
        rec = fixed("rec", [P, 2, 2, TB])
        lam2 = fixed("lam2", [P, 2])
        neglam = fixed("neglam", [P, 1])
        subg = fixed("subg", [P, 1])
        aneg = fixed("aneg", [P, 2 * SH])
        lamp = fixed("lamp", [P, 2, HD])
        ossq = fixed("ossq", [P, TB * HEADS])

        def const(name):
            return cst[:, CONST[name][0]:CONST[name][1]]

        def param(name, i=0, n=None):
            a = PARAM[name][0] + i
            return par[:, a:(PARAM[name][1] if n is None else a + n)]

        ident, tri_le, tri_ge, ones = const("ident"), const("tri_le"), const("tri_ge"), const("ones")

        arena = base[0]
        at = arena
        xbc, at = place(at, "xbc", [P, NXBC, SEQ])
        qk, at = place(at, "qk", [P, 2 * HEADS, SEQ])
        x_fwd, _ = place(at - 2 * HEADS * SEQ * 4, "x_fwd", [P, TB, INNER])
        attT, _ = place(at, "attT", [P, KD, SEQ])
        x_bwd, _ = place(at, "x_bwd", [P, TB, INNER])
        v_tok, at = place(at + KD * SEQ * 4, "v_tok", [P, TB, DM])
        zT, at = place(at, "zT", [P, XT, SEQ])
        gateT, at = place(at, "gateT", [P, 2 * KD, SEQ])
        temps = at
        m_mat, at = place(at, "m_mat", [P, 2, 6, HPG, P])
        cbm, at = place(at, "cbm", [P, 2, 6, P])
        a_tri, at = place(at, "a_tri", [P, 4, HPG, P])
        y_grp, at = place(at, "y_grp", [P, 2, TB, HPG * SP_])
        dt_v, at = place(at, "dt_v", [P, TB, 2 * SH])
        a_v, at = place(at, "a_v", [P, TB, 2 * SH])
        f_col, at = place(at, "f_col", [P, TB, 2 * SH])
        off_b, at = place(at, "off_b", [P, 2 * SH])
        sp, at2 = place(temps + 16384, "sp", [P, 6, TB * 2 * SH])
        c_tmp, at2 = place(at2, "c_tmp", [P, 2, 2, SEQ])
        xn, _ = place(temps, "xn", [P, TB, DM])
        rot_tmp, at2 = place(at2, "rot_tmp", [P, 2, SEQ])
        e_buf, a3 = place(temps, "e_buf", [P, 2, 2, TB, SEQ])
        wT, a3 = place(a3, "wT", [P, 2, TB, SEQ])
        o_sq, a3 = place(temps, "o_sq", [P, TB * HEADS, VD])
        s_tmp, a3 = place(temps, "s_tmp", [P, 4, SEQ])
        y_sq2, _ = place(temps, "y_sq2", [P, 2, 2, SEQ])
        r_bc, _ = place(temps + 8192, "r_bc", [P, SEQ])
        trig, _ = place(temps, "trig", [P, 4, SEQ])
        pos_i, _ = place(temps + 8192, "pos_i", [P, SEQ], I32)
        o_view = a_tri[:].rearrange("p t r l -> p (t r l)").rearrange("p (b h e) -> p b h e", b=TB, h=HEADS)

        at = arena
        ring, at = place(at, "ring", [P, RING, DM])
        sc, at = place(at, "sc", [P, TB, 2 * PH, PK])
        h2, at = place(at, "h2", [P, TB, DM])
        keys, at = place(at, "keys", [P, 2 * PH, PK])
        cand, at = place(at, "cand", [P, 2, TOPK, TOPK])
        eq, at = place(at, "eq", [P, 2, TOPK, TOPK])
        vals, at = place(at, "vals", [P, TB, 2 * PH, TOPK])
        idxs, at = place(at, "idxs", [P, TB, 2 * PH, TOPK], U32)
        g2row, at = place(at, "g2row", [P, DM])
        best, at = place(at, "best", [P, TB, PH, TOPK])
        posn, at = place(at, "posn", [P, TB, PH, TOPK], U32)
        idxf, at = place(at, "idxf", [P, 2 * PH, TOPK])
        ab_u, at = place(at, "ab_u", [P, 2, SLOTS], U32)
        ab_f, at = place(at, "ab_f", [P, 2, SLOTS])
        selv, at = place(at, "selv", [P, 2, SLOTS])
        ex_i, at = place(at, "ex_i", [P, TB, SLOTS], U32)
        gsum, at = place(at, "gsum", [P, TB, PH])
        gate_w, at = place(at, "gate_w", [P, TB, PH, TOPK])
        act_u, at = place(at, "act_u", [P, TB, SLOTS])
        stage, at = place(at, "stage", [P, 2, RING], U32)
        qryT, _ = place(at, "qryT", [P, 2 * PH, SEQ])
        gel, at = place(at, "gel", [P, TB, SLOTS])
        wgt, at = place(at, "wgt", [P, TB, SLOTS])
        diag, at = place(at, "diag", [P, 3, P])
        acc_v, at = place(at, "acc_v", [P, DM])

        bank = [ctx.enter_context(nc.psum_tensor(f"bank{i}", [P, 512], F32)) for i in range(8)]

        def two(b):
            return bank[b][:].rearrange("p (j t) -> p j t", j=2)

        def once(name):
            return ctx.enter_context(nc.semaphore(name))

        def sem(name, per_layer):
            return Count(once(name), per_layer)

        setup_loaded = once("setup_loaded")
        chunk_loaded = [sem(f"chunk_loaded{i}", 16 * CHUNKS // 2) for i in range(2)]
        chunk_begun = sem("chunk_begun", CHUNKS)
        tables_ready = once("tables_ready")
        trig_step = once("trig_step")
        trig_ready = once("trig_ready")
        par_ready = sem("par_ready", 1)
        x_ready = sem("x_ready", TB)
        alog_exp = sem("alog_exp", 1)
        sq_done = sem("sq_done", 2)
        ms_ready = sem("ms_ready", 2)
        rms_ready = sem("rms_ready", 2)
        xn_ready = sem("xn_ready", 2)
        bank_full = sem("bank_full", FILLS)
        bank_empty = sem("bank_empty", FILLS)
        conv_taps = sem("conv_taps", NXBC // 2 * CONV)
        xbc_ready = sem("xbc_ready", NXBC // 2)
        dt_proj = sem("dt_proj", 1)
        dt_act = sem("dt_act", 2)
        dt_abs_in = sem("dt_abs_in", 1)
        a_ready = sem("a_ready", 1)
        cums_done = sem("cums_done", 1)
        cums_copied = sem("cums_copied", 1)
        rot_full = sem("rot_full", HEADS)
        rot_empty = sem("rot_empty", HEADS)
        lam_in = sem("lam_in", 1)
        lam_exp = sem("lam_exp", 1)
        sc_done = sem("sc_done", HEADS)
        nb_ready = sem("nb_ready", HEADS)
        exp_done = sem("exp_done", HEADS)
        w_ready = sem("w_ready", HEADS)
        w_turned = sem("w_turned", HEADS)
        wT_ready = sem("wT_ready", HEADS)
        av_done = sem("av_done", HEADS)
        o_copied = sem("o_copied", HEADS)
        oms_ready = sem("oms_ready", 1)
        orms_ready = sem("orms_ready", 1)
        att_normed = sem("att_normed", 1)
        mix_full = sem("mix_full", 4 + 4 + 4)
        mix_empty = sem("mix_empty", 4 + 4 + 4)
        xt_full = sem("xt_full", 8)
        xt_empty = sem("xt_empty", 8)
        atri_ready = sem("atri_ready", 4 * GROUPS)
        f_done = sem("f_done", 4 * GROUPS)
        cb_done = sem("cb_done", GROUPS)
        diff_ready = sem("diff_ready", 4 * GROUPS)
        offexp_done = sem("offexp_done", 2 * GROUPS)
        cboff_copied = sem("cboff_copied", GROUPS)
        cb_masked = sem("cb_masked", GROUPS)
        dec_exp = sem("dec_exp", 4 * GROUPS)
        m_ready = sem("m_ready", GROUPS)
        y_done = sem("y_done", GROUPS)
        y_copied = sem("y_copied", GROUPS)
        y_turned = sem("y_turned", GROUPS)
        yz_ready = sem("yz_ready", GROUPS)
        ysq_ready = sem("ysq_ready", XT // 2)
        ysq_used = sem("ysq_used", XT // 2)
        yms_ready = sem("yms_ready", 1)
        yrms_ready = sem("yrms_ready", 1)
        m_scaled = sem("m_scaled", 1)
        peer_loaded = sem("peer_loaded", 32)
        h2_ready = sem("h2_ready", 1)
        best_shift = sem("best_shift", TB)
        best_exp = sem("best_exp", TB)
        experts_ready = sem("experts_ready", TB * PARTS)
        WAVES_LAYER = 2 * TB * WAVES
        staged = sem("staged", WAVES_LAYER)
        gathered = [sem(f"gathered{q}", 16 * QUAD * WAVES_LAYER) for q in range(QUADS)]
        quad_free = sem("quad_free", QUADS * WAVES_LAYER)
        gelu_done = sem("gelu_done", TB)
        wgt_ready = sem("wgt_ready", TB)
        diag_ready = sem("diag_ready", TB * 3 * QUADS * WAVES)
        diag_used = sem("diag_used", 2 + TB * 3 * QUADS * WAVES)
        dve_step = sem("dve_step", DVE_STEPS)
        out_ready = once("out_ready")
        fin_step = once("fin_step")
        fin_act = once("fin_act")
        stored = once("stored")

        block = ctx.enter_context(nc.Block())

        @block.sync
        def _(sync):
            sync.dma_start(cst[:], consts).then_inc(setup_loaded, 16)
            sync.dma_start(x_tok[:], x[0].rearrange("(b p) d -> p b d", p=P)).then_inc(setup_loaded, 16)
            sync.dma_start(par_all[:], params.rearrange("l p n -> p l n")).then_inc(setup_loaded, 16)
            sync.dma_start(pos_i[:], positions.broadcast_to([P, SEQ])).then_inc(setup_loaded, 16)
            sync.dma_start(wdt_all[:], w_dt.rearrange("l p n -> p l n")).then_inc(setup_loaded, 16)
            for s in range(2):
                sync.dma_start(w_ring[:, s, :], w_stream[s]).then_inc(chunk_loaded[s].sem, 16)
            with sync.Fori(0, DEPTH * CHUNKS // 2 - 1) as i:
                for s in range(2):
                    sync.wait_ge(chunk_begun.sem, 2 * i + s + 2)
                    sync.dma_start(w_ring[:, s, :], w_stream[bass.ds(2 * i + s + 2, 1)].rearrange("a p n -> p (a n)"))\
                        .then_inc(chunk_loaded[s].sem, 16)
            sync.wait_ge(out_ready, 1)
            sync.dma_start(out[0].rearrange("(b p) d -> p b d", p=P), h2[:]).then_inc(stored, 16)
            sync.wait_ge(stored, 16)

        @block.tensor
        def _(pe):
            def wait(sig, n, L):
                pe.wait_ge(sig.sem, sig.at(L, n))

            def wait_alone(sig, value):
                value = pe.to_reg(value)
                pe.wait_ge(setup_loaded, 80)
                pe.wait_ge(sig.sem, value)

            pe.wait_ge(setup_loaded, 80)
            with pe.Fori(0, DEPTH) as L:

                def chunk_wait(c):
                    wait(chunk_loaded[c % 2], 16 * (c // 2 + 1), L)

                def turn_normed(u):
                    wait(xn_ready, u + 1, L)
                    for j in range(4):
                        for k in (2 * j, 2 * j + 1):
                            for b in range(TB):
                                ins = pe.transpose(two(j)[:, k % 2, b * P:(b + 1) * P],
                                                   xn[:, b, k * P:(k + 1) * P], ident)
                        ins.then_inc(bank_full.sem, 1)

                def project(slot, rhs, b0, full, ks=KD, tiles=4, free=lambda j: None):
                    w = w_ring[:, slot, :].rearrange("p (k n) -> p k n", k=ks)
                    for j in range(tiles):
                        if j % 2 == 0:
                            free(j // 2)
                        for k in range(ks):
                            ins = pe.matmul(two(b0 + j // 2)[:, j % 2, :], w[:, k, j * P:(j + 1) * P],
                                            rhs(k), start=(k == 0), stop=(k == ks - 1))
                            if j == 0 and k == 0:
                                ins.then_inc(chunk_begun.sem, 1)
                        if j % 2 == 1:
                            ins.then_inc(full.sem, 1)

                def half(c, u, m):
                    if u == 0:
                        chunk_wait(c)
                    wait(bank_empty, m - 1, L)
                    w = w_ring[:, c % 2, :].rearrange("p (k n) -> p k n", k=KD)
                    for j in (2 * u, 2 * u + 1):
                        for k in range(KD):
                            ins = pe.matmul(two(m % 2)[:, j % 2, :], w[:, k, j * P:(j + 1) * P], hT[:, k, :],
                                            start=(k == 0), stop=(k == KD - 1))
                            if j == 0 and k == 0:
                                ins.then_inc(chunk_begun.sem, 1)
                    ins.then_inc(bank_full.sem, 1)

                turn_normed(0)
                wait_alone(bank_empty, bank_empty.at(L, 4))
                with pe.Fori(0, 2) as i:
                    for s in range(2):
                        pe.wait_ge(chunk_loaded[s].sem, chunk_loaded[s].at(L, 16 * (i + 1)))
                        w = w_ring[:, s, :].rearrange("p (k n) -> p k n", k=KD)
                        for j in range(4):
                            m = 2 * s + j // 2
                            if j % 2 == 0:
                                pe.wait_ge(bank_empty.sem, bank_empty.at(L, M_QK + 4 * i + m - 1))
                            for k in range(KD):
                                ins = pe.matmul(two(m % 2)[:, j % 2, :], w[:, k, j * P:(j + 1) * P], hT[:, k, :],
                                                start=(k == 0), stop=(k == KD - 1))
                                if j == 0 and k == 0:
                                    ins.then_inc(chunk_begun.sem, 1)
                            if j % 2 == 1:
                                ins.then_inc(bank_full.sem, 1)
                for c in range(2):
                    for i in range(4 * c, 4 * c + 4):
                        wait(bank_empty, M_QK + i + 1, L)
                        if i >= 4:
                            wait(rot_empty, i - 3, L)
                        pe.matmul(bank[4 + i % 4][:], const("prot"), qk[:, 2 * i:2 * i + 2, :], start=True, stop=True)\
                            .then_inc(rot_full.sem, 1)
                    chunk_wait(C_V + c)
                    w = w_ring[:, c, :].rearrange("p (k n) -> p k n", k=KD)
                    for b in range(TB):
                        m = M_V + 2 * c + b
                        wait(bank_empty, m - 1, L)
                        for k in range(KD):
                            ins = pe.matmul(bank[m % 2][:], hT[:, k, b * P:(b + 1) * P], w[:, k, :],
                                            start=(k == 0), stop=(k == KD - 1))
                            if b == 0 and k == 0:
                                ins.then_inc(chunk_begun.sem, 1)
                        ins.then_inc(bank_full.sem, 1)
                for b in range(TB):
                    for k in range(KD):
                        ins = pe.matmul(bank[3][:, b * 2 * SH:(b + 1) * 2 * SH], hT[:, k, b * P:(b + 1) * P],
                                        wdt_all[:, bass.ds(L, 1), k * 2 * SH:(k + 1) * 2 * SH], start=(k == 0), stop=(k == KD - 1))
                ins.then_inc(dt_proj.sem, 1)

                def scores(h):
                    if h == 0:
                        wait(rot_empty, HEADS, L)
                        wait(dt_abs_in, 1, L)
                    else:
                        wait(exp_done, h, L)
                    for c in range(2):
                        for b in range(TB):
                            ins = pe.matmul(two(2 + c)[:, b, :], qk[c * HD:(c + 1) * HD, h, b * P:(b + 1) * P],
                                            qk[c * HD:(c + 1) * HD, HEADS + h, :], start=True, stop=True)
                    ins.then_inc(sc_done.sem, 1)

                scores(0)
                for h in range(HEADS):
                    p = h % 2
                    if h + 1 < HEADS:
                        scores(h + 1)
                    half(C_XBC + h, 0, M_XBC + 2 * h)
                    wait(w_ready, h + 1, L)
                    if h >= 2:
                        wait(wT_ready, h - 1, L)
                    for kb in range(TB):
                        for b in range(TB):
                            ins = pe.transpose(two(4 + p)[:, kb, b * P:(b + 1) * P],
                                               e_buf[:, p, 0, b, kb * P:(kb + 1) * P], ident)
                    ins.then_inc(w_turned.sem, 1)
                    half(C_XBC + h, 1, M_XBC + 2 * h + 1)
                    wait(wT_ready, h + 1, L)
                    if h >= 2:
                        wait(o_copied, h - 1, L)
                    for b in range(TB):
                        for kb in range(TB):
                            ins = pe.matmul(bank[6 + p][:, b * VD:(b + 1) * VD], wT[:, p, kb, b * P:(b + 1) * P],
                                            v_tok[:, kb, h * VD:(h + 1) * VD], start=(kb == 0), stop=(kb == TB - 1))
                    ins.then_inc(av_done.sem, 1)
                for c in range(2):
                    for u in range(2):
                        half(C_GATT + c, u, M_GATT + 2 * c + u)
                wait(a_ready, 1, L)
                wait(exp_done, HEADS, L)
                for b in range(TB):
                    pe.matmul(bank[3][:, b * 64:b * 64 + SH], tri_le, a_v[:, b, 0:SH], start=True, stop=True)
                    pe.matmul(bank[3][:, b * 64 + SH:(b + 1) * 64], tri_ge, a_v[:, b, SH:2 * SH], start=True, stop=True)
                    ins = pe.matmul(bank[3][:, 128 + b * 64:128 + (b + 1) * 64], ones, a_v[:, b, :],
                                    start=True, stop=True)
                ins.then_inc(cums_done.sem, 1)
                wait(att_normed, 1, L)
                wait(wT_ready, HEADS, L)
                for j in range(4):
                    for h in (2 * j, 2 * j + 1):
                        for b in range(TB):
                            ins = pe.transpose(two(4 + j)[:, h % 2, b * P:(b + 1) * P], o_view[:, b, h, :], ident)
                    ins.then_inc(bank_full.sem, 1)
                wait(bank_empty, M_ATT + 4, L)
                wait(cums_copied, 1, L)
                for c in range(2):
                    chunk_wait(C_ATT + c)
                    project(c % 2, lambda k: attT[:, k, :], 2 * c, mix_full)

                def turn_x(i):
                    b, c = divmod(i, 4)
                    if i >= 4:
                        wait(xt_empty, i - 3, L)
                    for j in range(4):
                        ins = pe.transpose(bank[4 + i % 4][:, j * P:(j + 1) * P], xbc[:, 4 * c + j, b * P:(b + 1) * P],
                                           ident)
                    ins.then_inc(xt_full.sem, 1)

                def decay(g, t):
                    wait(atri_ready, 4 * g + t + 1, L)
                    if 4 * g + t >= 2:
                        wait(diff_ready, 4 * g + t - 1, L)
                    if t == 3:
                        wait(offexp_done, 2 * g + 1, L)
                    if t == 0 and g > 0:
                        wait(offexp_done, 2 * g, L)
                    pe.matmul(bank[2 + t % 2][:], ones, a_tri[:, t, :, :], start=True, stop=True)\
                        .then_inc(f_done.sem, 1)

                def c_times_b(g):
                    if g > 0:
                        wait(cb_masked, g, L)
                        wait(cboff_copied, g, L)
                    for s in range(TB):
                        ins = pe.matmul(two(4)[:, s, :], xbc[:, XT + g, s * P:(s + 1) * P], xbc[:, XT + GROUPS + g, :],
                                        start=True, stop=True)
                    ins.then_inc(cb_done.sem, 1)

                wait(xbc_ready, NXBC // 2, L)
                for i in range(4):
                    turn_x(i)
                wait(mix_empty, 4, L)
                half(C_Z, 0, M_Z)
                for i in range(4, 8):
                    turn_x(i)
                half(C_Z, 1, M_Z + 1)
                decay(0, 0)
                decay(0, 1)
                decay(0, 2)
                decay(0, 3)
                wait(xt_empty, 8, L)
                c_times_b(0)
                beside = [C_Z + 1, C_Z + 2, C_Z + 3, C_GSSM, C_GSSM + 1]
                for g in range(GROUPS):
                    p = g % 2
                    if g + 1 < GROUPS:
                        decay(g + 1, 0)
                        decay(g + 1, 1)
                    if g < len(beside):
                        half(beside[g], 0, M_Z + 2 + 2 * g)
                    if g + 1 < GROUPS:
                        decay(g + 1, 2)
                        decay(g + 1, 3)
                        c_times_b(g + 1)
                    wait(m_ready, g + 1, L)
                    if g >= 2:
                        wait(y_copied, g - 1, L)
                    for l in range(TB):
                        terms = [(0, 0, x_fwd), (2, 0, x_bwd), (5, 1, x_bwd)] if l == 0 else \
                                [(1, 1, x_fwd), (3, 1, x_bwd), (4, 0, x_fwd)]
                        for r in range(HPG):
                            h = HPG * g + r
                            col = l * HPG * SP_ + r * SP_
                            for n, (t, s, xs) in enumerate(terms):
                                ins = pe.matmul(bank[5 + p][:, col:col + SP_], m_mat[:, p, t, r, :],
                                                xs[:, s, h * SP_:(h + 1) * SP_], start=(n == 0), stop=(n == 2))
                    ins.then_inc(y_done.sem, 1)
                    if g < len(beside):
                        half(beside[g], 1, M_Z + 3 + 2 * g)
                    wait(y_copied, g + 1, L)
                    if g >= 1:
                        wait(yz_ready, g, L)
                    for j in range(2):
                        for l in range(TB):
                            ins = pe.transpose(two(7)[:, j, l * P:(l + 1) * P], y_grp[:, p, l, j * P:(j + 1) * P], ident)
                    ins.then_inc(y_turned.sem, 1)
                for i in range(XT // 2):
                    wait(ysq_ready, i + 1, L)
                    for u in range(2):
                        ins = pe.matmul(bank[4][:, 0:SEQ], ones, y_sq2[:, i % 2, u, :],
                                        start=(i == 0 and u == 0), stop=(i == XT // 2 - 1 and u == 1))
                    ins.then_inc(ysq_used.sem, 1)
                wait(m_scaled, 1, L)
                wait(bank_empty, M_GSSM + 4, L)
                for c in range(4):
                    chunk_wait(C_SSM + c)
                    project(c % 2, lambda k: zT[:, k, :], c, mix_full, ks=XT, tiles=2)
                wait(mix_empty, 8, L)
                for c in range(2):
                    chunk_wait(C_OUT + c)
                    w = w_ring[:, c, :].rearrange("p (k n) -> p k n", k=KD)
                    for b in range(TB):
                        for k in range(KD):
                            ins = pe.matmul(bank[2 * c + b][:], gateT[:, k, b * P:(b + 1) * P], w[:, k, :],
                                            start=(k == 0), stop=(k == KD - 1))
                            if b == 0 and k == 0:
                                ins.then_inc(chunk_begun.sem, 1)
                        ins.then_inc(mix_full.sem, 1)

                turn_normed(1)
                wait(bank_empty, M_ROUTE, L)
                for kind, i, *block_of in ROUTE_FILLS:
                    if kind == "q":
                        c, u = divmod(i, 2)
                        if u == 0:
                            chunk_wait(C_WQ + c)
                        wait(bank_empty, FILL["q", i - 2] + 1 if i >= 2 else M_ROUTE, L)
                        w = w_ring[:, c % 2, :].rearrange("p (k n) -> p k n", k=KD)
                        for j in (2 * u, 2 * u + 1):
                            for k in range(KD):
                                ins = pe.matmul(two(i % 2)[:, j % 2, :], w[:, k, j * P:(j + 1) * P], hT[:, k, :],
                                                start=(k == 0), stop=(k == KD - 1))
                                if j == 0 and k == 0:
                                    ins.then_inc(chunk_begun.sem, 1)
                        ins.then_inc(bank_full.sem, 1)
                    else:
                        b = block_of[0]
                        if i == 0 and b == 0:
                            wait(peer_loaded, 32, L)
                        wait(bank_empty, FILL["q", 2 * i + 1] + 1, L)
                        for j in range(4):
                            t = 4 * i + j
                            ins = pe.matmul(bank[2 + b][:, j * PK:(j + 1) * PK], qryT[:, t, b * P:(b + 1) * P],
                                            keys[:, t, :], start=True, stop=True)
                        ins.then_inc(bank_full.sem, 1)

                for b in range(TB):
                    b0 = 4 + 2 * b
                    if b == 0:
                        wait(bank_empty, FILLS, L)
                    for n in range(2):
                        ins = pe.matmul(bank[b0 + n][:], ident, x_tok[:, b, n * 512:(n + 1) * 512], start=True,
                                        stop=False, skip_group_check=True)
                        if b == 0:
                            ins.then_inc(diag_used.sem, 1)
                    with pe.Fori(0, WAVES) as w:
                        for q in range(QUADS):
                            pe.wait_ge(gathered[q].sem,
                                       gathered[q].at(L, 16 * QUAD * (WAVES * (2 * b + 1) + w + 1)))
                            for s in range(3):
                                pe.wait_ge(diag_ready.sem, diag_ready.at(L, 3 * (QUADS * (WAVES * b + w) + q) + s + 1))
                                for n in range(2):
                                    ins = pe.matmul(bank[b0 + n][:], diag[:, s, :],
                                                    ring[:, QUAD * q + s, n * 512:(n + 1) * 512],
                                                    start=False, stop=True, skip_group_check=True)
                                ins.then_inc(diag_used.sem, 1)

        @block.scalar
        def _(act):
            def wait(sig, n, L):
                act.wait_ge(sig.sem, sig.at(L, n))

            def wait_alone(sig, value):
                value = act.to_reg(value)
                act.wait_ge(setup_loaded, 80)
                act.wait_ge(sig.sem, value)

            def squares(u, L):
                for b in range(TB):
                    ins = act.activation(xn[:, b, :], x_tok[:, b, :], ACT.Square, accum_out=ssq[:, b:b + 1])
                ins.then_inc(sq_done.sem, 1)
                wait(ms_ready, u + 1, L)
                act.activation(rms[:], rms[:], ACT.Sqrt).then_inc(rms_ready.sem, 1)

            def gained(m0, gain, L):
                for j in range(4):
                    wait(bank_full, m0 + j + 1, L)
                    for k in (2 * j, 2 * j + 1):
                        ins = act.activation(hT[:, k, :], two(j)[:, k % 2, :], ACT.Copy, scale=param(gain, k, 1))
                    ins.then_inc(bank_empty.sem, 1)

            act.wait_ge(setup_loaded, 80)
            act.wait_ge(trig_ready, 1)
            act.activation(sin_t[:], trig[:, 2, :], ACT.Sin)
            act.activation(cos_t[:], trig[:, 3, :], ACT.Sin).then_inc(tables_ready, 1)

            act.wait_ge(tables_ready, 1)

            with act.Fori(0, DEPTH) as L:
                wait(x_ready, 1, L)
                squares(0, L)
                wait(par_ready, 1, L)
                act.activation(aneg[:], param("alog"), ACT.Exp).then_inc(alog_exp.sem, 1)
                gained(0, "n1g", L)
                for i in range(8):
                    wait(bank_full, M_QK + i + 1, L)
                    act.activation(qk[:, 2 * i:2 * i + 2, :], two(i % 2), ACT.Copy).then_inc(bank_empty.sem, 1)
                for i in range(4):
                    c, b = divmod(i, 2)
                    wait(bank_full, M_V + i + 1, L)
                    act.activation(v_tok[:, b, c * 512:(c + 1) * 512], bank[i % 2][:], ACT.Copy).then_inc(bank_empty.sem, 1)
                wait(lam_in, 1, L)
                act.activation(lam2[:], lam2[:], ACT.Exp).then_inc(lam_exp.sem, 1)
                wait(dt_abs_in, 1, L)
                act.activation(sp[:, 1, :], sp[:, 0, :], ACT.Abs).then_inc(dt_act.sem, 1)
                wait(dt_act, 1, L)
                act.activation(sp[:, 1, :], sp[:, 1, :], ACT.Exp, scale=-1.0).then_inc(dt_act.sem, 1)

                def exps(h):
                    p = h % 2
                    wait(nb_ready, h + 1, L)
                    if h >= 2:
                        wait(w_turned, h - 1, L)
                    for c in range(2):
                        for b in range(TB):
                            ins = act.activation(e_buf[:, p, c, b, :], two(2 + c)[:, b, :], ACT.Exp,
                                                 bias=nb[:, p, c, b:b + 1], scale=HD ** -0.5,
                                                 accum_out=sums[:, p, c, b:b + 1])
                    ins.then_inc(exp_done.sem, 1)

                def raw(j):
                    wait(bank_full, M_XBC + j + 1, L)
                    act.activation(xbc[:, 2 * j:2 * j + 2, :], two(j % 2), ACT.Copy).then_inc(bank_empty.sem, 1)

                def silu(j):
                    wait(conv_taps, CONV * (j + 1), L)
                    act.activation(xbc[:, 2 * j:2 * j + 2, :], c_tmp[:, j % 2], ACT.Silu).then_inc(xbc_ready.sem, 1)

                exps(0)
                for h in range(HEADS):
                    p = h % 2
                    if h + 1 < HEADS:
                        exps(h + 1)
                    if h >= 1:
                        silu(2 * h - 1)
                    raw(2 * h)
                    wait(w_turned, h + 1, L)
                    if h >= 2:
                        wait(av_done, h - 1, L)
                    act.activation(wT[:, p], two(4 + p), ACT.Copy).then_inc(wT_ready.sem, 1)
                    raw(2 * h + 1)
                    silu(2 * h)
                silu(2 * HEADS - 1)

                def gate(m, tile):
                    wait(bank_full, m + 1, L)
                    for j in range(2):
                        ins = act.activation(gateT[:, tile + j, :], two(m % 2)[:, j, :], ACT.Sigmoid,
                                             bias=param("gb", tile + j, 1))
                    ins.then_inc(bank_empty.sem, 1)

                gate(M_GATT, 0)
                wait(oms_ready, 1, L)
                act.activation(ossq[:], ossq[:], ACT.Sqrt).then_inc(orms_ready.sem, 1)
                for i in range(1, 4):
                    gate(M_GATT + i, 2 * i)
                for j in range(4):
                    wait(bank_full, M_ATT + j + 1, L)
                    act.activation(attT[:, 2 * j:2 * j + 2, :], two(4 + j), ACT.Copy, scale=subg[:, 0:1])\
                        .then_inc(bank_empty.sem, 1)

                def aside(m):
                    if m >= M_GSSM:
                        gate(m, KD + 2 * (m - M_GSSM))
                        return
                    i = m - M_Z
                    wait(bank_full, m + 1, L)
                    act.activation(zT[:, 2 * i:2 * i + 2, :], two(i % 2), ACT.Silu).then_inc(bank_empty.sem, 1)

                def copy_y(g):
                    wait(y_done, g + 1, L)
                    if g >= 2:
                        wait(y_turned, g - 1, L)
                    act.activation(y_grp[:, g % 2], bank[5 + g % 2][:].rearrange("p (l n) -> p l n", l=TB), ACT.Copy)\
                        .then_inc(y_copied.sem, 1)

                def block_exps(g, ts):
                    for t in ts:
                        wait(diff_ready, 4 * g + t + 1, L)
                        act.activation(m_mat[:, g % 2, t], m_mat[:, g % 2, t], ACT.Exp).then_inc(dec_exp.sem, 1)

                def cross_exps(g, t):
                    src, col = (1, HPG * g) if t == 4 else (2, SH + HPG * g)
                    if g >= 2 and t == 4:
                        wait(y_done, g - 1, L)
                    wait(diff_ready, 4 * g + src + 1, L)
                    for r in range(HPG):
                        ins = act.activation(m_mat[:, g % 2, t, r, :], bank[2 + src % 2][:, r * P:(r + 1) * P], ACT.Exp,
                                             bias=off_b[:, col + r:col + r + 1])
                    ins.then_inc(offexp_done.sem, 1)

                def cross_cb(g):
                    wait(cb_masked, g + 1, L)
                    if g >= 2:
                        wait(m_ready, g - 1, L)
                    act.activation(cbm[:, g % 2, 4:6, :], bank[4][:, P:3 * P].rearrange("p (t l) -> p t l", t=2), ACT.Copy)\
                        .then_inc(cboff_copied.sem, 1)

                aside(M_Z)
                aside(M_Z + 1)
                cross_exps(0, 4)
                block_exps(0, (0, 1))
                cross_exps(0, 5)
                block_exps(0, (2, 3))
                cross_cb(0)
                for g in range(GROUPS):
                    if g + 1 < GROUPS:
                        cross_exps(g + 1, 4)
                        block_exps(g + 1, (0, 1))
                    if g < 5:
                        aside(M_Z + 2 + 2 * g)
                    if g + 1 < GROUPS:
                        cross_exps(g + 1, 5)
                        block_exps(g + 1, (2, 3))
                        cross_cb(g + 1)
                    copy_y(g)
                    if g < 5:
                        aside(M_Z + 3 + 2 * g)
                for i in range(XT // 2):
                    wait(yz_ready, min(GROUPS, i + 1), L)
                    if i >= 2:
                        wait(ysq_used, i - 1, L)
                    act.activation(y_sq2[:, i % 2], zT[:, 2 * i:2 * i + 2, :], ACT.Square).then_inc(ysq_ready.sem, 1)
                wait(yms_ready, 1, L)
                act.activation(r_bc[:], r_bc[:], ACT.Sqrt).then_inc(yrms_ready.sem, 1)

                wait(mix_empty, 12, L)
                act.dma_start(keys[:], keys_t[bass.ds(L, 1)].rearrange("a p (t k) -> p (a t) k", k=PK))\
                    .then_inc(peer_loaded.sem, 16)
                act.dma_start(g2row[:], norm2_rows[bass.ds(L, 1)].broadcast_to([P, DM])).then_inc(peer_loaded.sem, 16)
                squares(1, L)
                gained(M_NORM2, "n2g", L)
                wait(h2_ready, 1, L)
                for kind, i, *block_of in ROUTE_FILLS:
                    if kind == "q":
                        wait(bank_full, FILL["q", i] + 1, L)
                        act.activation(qryT[:, 2 * i:2 * i + 2, :], two(i % 2), ACT.Copy).then_inc(bank_empty.sem, 1)
                    else:
                        b = block_of[0]
                        wait(bank_full, FILL["s", i, b] + 1, L)
                        act.activation(sc[:, b, 4 * i:4 * i + 4, :], bank[2 + b][:].rearrange("p (t k) -> p t k", k=PK),
                                       ACT.Copy).then_inc(bank_empty.sem, 1)

                for b in range(TB):
                    wait(best_shift, b + 1, L)
                    act.activation(gate_w[:, b], gate_w[:, b], ACT.Exp).then_inc(best_exp.sem, 1)
                    wait(quad_free, QUADS * WAVES * (2 * b + 1), L)
                    act.activation(gel[:, b, :], act_u[:, b, :], ACT.Gelu).then_inc(gelu_done.sem, 1)
                    wait(wgt_ready, b + 1, L)
                    with act.Fori(0, WAVES) as w:
                        for q in range(QUADS):
                            for s in range(3):
                                n = 3 * (QUADS * (WAVES * b + w) + q) + s
                                wait_alone(diag_used, diag_used.at(L, n + 1))
                                act.activation(diag[:, s, :], ident, ACT.Copy,
                                               scale=wgt[:, b, bass.ds(RING * w + QUAD * q + s, 1)])\
                                    .then_inc(diag_ready.sem, 1)

            wait(x_ready, 1, DEPTH)
            act.dma_start(g2row[:], final_row.broadcast_to([P, DM])).then_inc(peer_loaded.sem, 16)
            squares(0, DEPTH)

        @block.vector
        def _(dve):
            def wait(sig, n, L):
                dve.wait_ge(sig.sem, sig.at(L, n))

            def wait_alone(sig, value):
                value = dve.to_reg(value)
                dve.wait_ge(setup_loaded, 80)
                dve.wait_ge(sig.sem, value)

            dve.wait_ge(setup_loaded, 80)
            done = [0]

            def trig_do(ins):
                done[0] += 1
                ins.then_inc(trig_step, 1)
                dve.wait_ge(trig_step, done[0])

            MAGIC = 1.5 * 2.0 ** 23
            T1 = 6.28125
            T2 = math.floor((2 * math.pi - T1) * 2 ** 20) / 2 ** 20
            T3 = 2 * math.pi - T1 - T2
            trig_do(dve.tensor_copy(trig[:, 0, :], pos_i[:]))
            trig_do(dve.tensor_scalar(trig[:, 0, :], trig[:, 0, :], const("freq"), None, ALU.mult))
            for side, quarter in ((2, 0.0), (3, 0.25)):
                trig_do(dve.tensor_scalar(trig[:, 1, :], trig[:, 0, :], 1.0 / (2 * math.pi), quarter, ALU.mult, ALU.add))
                trig_do(dve.tensor_scalar(trig[:, 1, :], trig[:, 1, :], MAGIC, None, ALU.add))
                trig_do(dve.tensor_scalar(trig[:, 1, :], trig[:, 1, :], -MAGIC, None, ALU.add))
                for n, t in enumerate((T1, T2, T3)):
                    trig_do(dve.scalar_tensor_tensor(out=trig[:, side, :], in0=trig[:, 1, :], scalar=-t,
                                                     in1=trig[:, 0 if n == 0 else side, :], op0=ALU.mult, op1=ALU.add))
                if quarter:
                    trig_do(dve.tensor_scalar(trig[:, side, :], trig[:, side, :], math.pi / 2, None, ALU.add))
                trig_do(dve.tensor_scalar(trig[:, side, :], trig[:, side, :], 3.1415925, -3.1415925, ALU.min, ALU.max))
            dve.nop().then_inc(trig_ready, 1)
            dve.nop().then_inc(x_ready.sem, 1)

            with dve.Fori(0, DEPTH) as L:
                st = Steps(dve, dve_step, L)

                def step(ins):
                    st.do(ins)
                    st.wait()

                def step_alone(ins):
                    st.do(ins)
                    wait_alone(dve_step, dve_step.at(L, st.n))

                def normed(u):
                    wait(sq_done, u + 1, L)
                    dve.tensor_scalar(rms[:], ssq[:], 1.0 / DM, EPS, ALU.mult, ALU.add).then_inc(ms_ready.sem, 1)
                    wait(rms_ready, u + 1, L)
                    step(dve.reciprocal(rstd[:], rms[:]))
                    for b in range(TB):
                        ins = dve.tensor_scalar(xn[:, b, :], x_tok[:, b, :], rstd[:, b:b + 1], None, ALU.mult)
                    ins.then_inc(xn_ready.sem, 1)

                wait(x_ready, 1, L)
                dve.tensor_copy(par[:], par_all[:, bass.ds(L, 1), :].rearrange("p a n -> p (a n)"))\
                    .then_inc(par_ready.sem, 1)
                wait(par_ready, 1, L)
                lam4 = param("lam").rearrange("p (n c d) -> p n c d", n=2, c=2)
                step(dve.tensor_tensor(lamp[:], lam4[:, :, 0, :], lam4[:, :, 1, :], ALU.mult))
                dve.tensor_reduce(lam2[:], lamp[:], AX.X, ALU.add).then_inc(lam_in.sem, 1)
                step(dve.tensor_scalar(subg[:], param("laminit"), -1.0, 1.0, ALU.mult, ALU.add))
                step(dve.tensor_tensor(subg[:], subg[:], param("sub"), ALU.mult))
                normed(0)
                wait(alog_exp, 1, L)
                step_alone(dve.tensor_scalar(aneg[:], aneg[:], -1.0, None, ALU.mult))

                dve.wait_ge(tables_ready, 1)
                for i in range(HEADS):
                    wait(rot_full, i + 1, L)
                    if i >= 1:
                        wait(rot_empty, i, L)
                    pair = qk[:, 2 * i:2 * i + 2, :]
                    dve.tensor_tensor(rot_tmp[:], two(4 + i % 4), bc(sin_t[:], 1, 2), ALU.mult)
                    step(dve.tensor_tensor(pair, pair, bc(cos_t[:], 1, 2), ALU.mult))
                    dve.tensor_tensor(pair, pair, rot_tmp[:], ALU.add).then_inc(rot_empty.sem, 1)

                wait(dt_proj, 1, L)
                dve.tensor_tensor(sp[:, 0, :].rearrange("p (b n) -> p b n", b=TB),
                                  bank[3][:, 0:2 * 2 * SH].rearrange("p (b n) -> p b n", b=TB),
                                  bc(param("dtb"), 1, TB), ALU.add).then_inc(dt_abs_in.sem, 1)
                wait(dt_act, 2, L)
                step(dve.tensor_scalar(sp[:, 2, :], sp[:, 1, :], 2.0, None, ALU.add))
                step(dve.reciprocal(sp[:, 2, :], sp[:, 2, :]))
                step(dve.tensor_tensor(sp[:, 1, :], sp[:, 1, :], sp[:, 2, :], ALU.mult))
                step(dve.tensor_tensor(sp[:, 3, :], sp[:, 1, :], sp[:, 1, :], ALU.mult))
                step(dve.tensor_scalar(sp[:, 4, :], sp[:, 3, :], LOG_TERMS[0], None, ALU.mult))
                for c in LOG_TERMS[1:]:
                    step(dve.scalar_tensor_tensor(out=sp[:, 4, :], in0=sp[:, 4, :], scalar=c, in1=sp[:, 3, :],
                                                  op0=ALU.add, op1=ALU.mult))
                step(dve.scalar_tensor_tensor(out=sp[:, 4, :], in0=sp[:, 4, :], scalar=1.0, in1=sp[:, 1, :],
                                              op0=ALU.add, op1=ALU.mult))
                step(dve.tensor_scalar(sp[:, 5, :], sp[:, 0, :], 0.0, None, ALU.max))
                step(dve.scalar_tensor_tensor(out=dt_v[:].rearrange("p b n -> p (b n)"), in0=sp[:, 4, :], scalar=2.0,
                                              in1=sp[:, 5, :], op0=ALU.mult, op1=ALU.add))
                dve.tensor_tensor(a_v[:], dt_v[:], bc(aneg[:], 1, TB), ALU.mult).then_inc(a_ready.sem, 1)

                wait(lam_exp, 1, L)
                step(dve.tensor_tensor(neglam[:], lam2[:, 1:2], lam2[:, 0:1], ALU.subtract))
                step(dve.tensor_tensor(neglam[:], neglam[:], param("laminit"), ALU.subtract))

                def maxima(h):
                    p = h % 2
                    wait(sc_done, h + 1, L)
                    for c in range(2):
                        ins = dve.tensor_reduce(mx[:, p, c, :], two(2 + c), AX.X, ALU.max)
                    step(ins)
                    dve.tensor_scalar(nb[:, p], mx[:, p], -HD ** -0.5, None, ALU.mult).then_inc(nb_ready.sem, 1)

                def convolve(j):
                    wait(bank_empty, M_XBC + j + 1, L)
                    for n, tap in enumerate((2, 0, 1, 3, 4)):
                        lo, hi = max(0, 2 - tap), SEQ - max(0, tap - 2)
                        for v in range(2):
                            tile = 2 * j + v
                            src = xbc[:, tile, lo + tap - 2:hi + tap - 2]
                            dst = c_tmp[:, j % 2, v, lo:hi]
                            w = param("cw", CONV * tile + tap, 1)
                            if n == 0:
                                ins = dve.tensor_scalar(dst, src, w, param("cb", tile, 1), ALU.mult, ALU.add)
                            else:
                                ins = dve.scalar_tensor_tensor(out=dst, in0=src, scalar=w, in1=dst,
                                                               op0=ALU.mult, op1=ALU.add)
                        ins.then_inc(conv_taps.sem, 1)
                        if n < CONV - 1:
                            wait(conv_taps, CONV * j + n + 1, L)

                def weights(h):
                    p = h % 2
                    wait(exp_done, h + 1, L)
                    step(dve.reciprocal(rec[:, p], sums[:, p]))
                    step(dve.tensor_scalar(rec[:, p, 1, :], rec[:, p, 1, :], neglam[:, 0:1], None, ALU.mult))
                    for b in range(TB):
                        ins = dve.tensor_scalar(e_buf[:, p, 0, b, :], e_buf[:, p, 0, b, :], rec[:, p, 0, b:b + 1], None,
                                                ALU.mult)
                    step(ins)
                    for b in range(TB):
                        ins = dve.scalar_tensor_tensor(out=e_buf[:, p, 0, b, :], in0=e_buf[:, p, 1, b, :],
                                                       scalar=rec[:, p, 1, b:b + 1], in1=e_buf[:, p, 0, b, :],
                                                       op0=ALU.mult, op1=ALU.add)
                    ins.then_inc(w_ready.sem, 1)

                def copy_o(h):
                    wait(av_done, h + 1, L)
                    dve.tensor_copy(o_view[:, :, h, :], bank[6 + h % 2][:, 0:TB * VD].rearrange("p (b e) -> p b e", b=TB))\
                        .then_inc(o_copied.sem, 1)

                maxima(0)
                weights(0)
                for h in range(HEADS):
                    if h + 1 < HEADS:
                        maxima(h + 1)
                    convolve(2 * h)
                    if h + 1 < HEADS:
                        weights(h + 1)
                    convolve(2 * h + 1)
                    copy_o(h)
                wait(o_copied, HEADS, L)
                o16 = o_view.rearrange("p b h e -> p (b h) e")
                step(dve.tensor_tensor(o_sq[:], o16, o16, ALU.mult))
                step(dve.tensor_reduce(ossq[:], o_sq[:], AX.X, ALU.add))
                dve.tensor_scalar(ossq[:], ossq[:], 1.0 / VD, EPS, ALU.mult, ALU.add).then_inc(oms_ready.sem, 1)
                wait(orms_ready, 1, L)
                step(dve.reciprocal(ossq[:], ossq[:]))
                dve.tensor_tensor(o16, o16, bc(ossq[:], 2, VD), ALU.mult).then_inc(att_normed.sem, 1)
                wait(cums_done, 1, L)
                step(dve.tensor_copy(f_col[:].rearrange("p b n -> p (b n)"), bank[3][:, 0:128]))
                dve.tensor_tensor(off_b[:, 0:SH], bank[3][:, 128:128 + SH], f_col[:, 0, 0:SH], ALU.subtract)
                dve.tensor_tensor(off_b[:, SH:2 * SH], bank[3][:, 192 + SH:192 + 2 * SH], f_col[:, 1, SH:2 * SH],
                                  ALU.subtract).then_inc(cums_copied.sem, 1)
                wait(bank_empty, M_ATT, L)
                for i in range(4):
                    wait(mix_full, i + 1, L)
                    g = gateT[:, 2 * i:2 * i + 2, :]
                    dve.tensor_tensor(g, two(i), g, ALU.mult).then_inc(mix_empty.sem, 1)

                for i in range(8):
                    b, c = divmod(i, 4)
                    wait(xt_full, i + 1, L)
                    for d, xs in enumerate((x_fwd, x_bwd)):
                        ins = dve.tensor_tensor(xs[:, b, c * 512:(c + 1) * 512].rearrange("p (h n) -> p h n", n=SP_),
                                                bank[4 + i % 4][:].rearrange("p (h n) -> p h n", n=SP_),
                                                bc(dt_v[:, b, d * SH + 8 * c:d * SH + 8 * c + 8], 2, SP_), ALU.mult)
                    ins.then_inc(xt_empty.sem, 1)

                blocks = bank[4][:].rearrange("p (a l) -> p a l", l=P)

                def differences(g, ts):
                    p = g % 2
                    if g >= 2 and ts[0] == 0:
                        wait(y_done, g - 1, L)
                    for t in ts:
                        d, b = divmod(t, 2)
                        wait(f_done, 4 * g + t + 1, L)
                        for r in range(HPG):
                            col = d * SH + HPG * g + r
                            ins = dve.tensor_scalar(m_mat[:, p, t, r, :], bank[2 + t % 2][:, r * P:(r + 1) * P],
                                                    f_col[:, b, col:col + 1], 0.0, ALU.subtract, ALU.min)
                        ins.then_inc(diff_ready.sem, 1)

                def decay_times_cb(g):
                    p = g % 2
                    wait(cb_done, g + 1, L)
                    dve.tensor_tensor(cbm[:, p, 0:2, :], blocks[:, 0:4:3, :], bc(tri_le, 1, 2), ALU.mult)
                    dve.tensor_tensor(cbm[:, p, 2:4, :], blocks[:, 0:4:3, :], bc(tri_ge, 1, 2), ALU.mult)\
                        .then_inc(cb_masked.sem, 1)
                    wait(cb_masked, g + 1, L)
                    for t in range(4):
                        wait(dec_exp, 4 * g + t + 1, L)
                        dve.tensor_tensor(m_mat[:, p, t], m_mat[:, p, t], bc(cbm[:, p, t, :], 1, HPG), ALU.mult)
                    wait(offexp_done, 2 * g + 2, L)
                    wait(cboff_copied, g + 1, L)
                    dve.tensor_tensor(m_mat[:, p, 4:6], m_mat[:, p, 4:6], bc(cbm[:, p, 4:6, :], 2, HPG), ALU.mult)\
                        .then_inc(m_ready.sem, 1)

                def skip_and_gate(g):
                    wait(y_turned, g + 1, L)
                    for j in range(2):
                        t = 2 * g + j
                        ins = dve.scalar_tensor_tensor(out=xbc[:, t, :], in0=xbc[:, t, :], scalar=param("dsk", t, 1),
                                                       in1=two(7)[:, j, :], op0=ALU.mult, op1=ALU.add)
                    step(ins)
                    wait(bank_empty, M_Z + g + 1, L)
                    zs = zT[:, 2 * g:2 * g + 2, :]
                    dve.tensor_tensor(zs, zs, xbc[:, 2 * g:2 * g + 2, :], ALU.mult).then_inc(yz_ready.sem, 1)

                differences(0, (0, 1))
                differences(0, (2, 3))
                decay_times_cb(0)
                for g in range(GROUPS):
                    if g + 1 < GROUPS:
                        differences(g + 1, (0, 1))
                    if g >= 1:
                        skip_and_gate(g - 1)
                    if g + 1 < GROUPS:
                        differences(g + 1, (2, 3))
                        decay_times_cb(g + 1)
                skip_and_gate(GROUPS - 1)
                wait(yz_ready, GROUPS, L)
                for t in range(XT):
                    wait(ysq_ready, t // 2 + 1, L)
                    ins = dve.tensor_scalar(zT[:, t, :], zT[:, t, :], param("sng", t, 1), None, ALU.mult)
                ins.then_inc(m_scaled.sem, 1)
                wait(ysq_used, XT // 2, L)
                dve.tensor_scalar(r_bc[:], bank[4][:, 0:SEQ], 1.0 / INNER, EPS, ALU.mult, ALU.add)\
                    .then_inc(yms_ready.sem, 1)
                wait(yrms_ready, 1, L)
                wait(bank_empty, M_NORM2, L)
                step(dve.reciprocal(r_bc[:], r_bc[:]))
                step(dve.tensor_tensor(gateT[:, KD:2 * KD, :], gateT[:, KD:2 * KD, :], bc(r_bc[:], 1, KD), ALU.mult))
                for i in range(4):
                    wait(mix_full, 4 + i + 1, L)
                    step(dve.tensor_tensor(s_tmp[:, 0:2, :], two(i), gateT[:, KD + 2 * i:KD + 2 * i + 2, :], ALU.mult))
                    g = gateT[:, 2 * i:2 * i + 2, :]
                    dve.tensor_tensor(g, g, s_tmp[:, 0:2, :], ALU.add).then_inc(mix_empty.sem, 1)
                    wait(mix_empty, 4 + i + 1, L)
                for i in range(4):
                    c, b = divmod(i, 2)
                    wait(mix_full, 8 + i + 1, L)
                    xs = x_tok[:, b, c * 512:(c + 1) * 512]
                    dve.tensor_tensor(xs, bank[i][:], xs, ALU.add).then_inc(mix_empty.sem, 1)

                normed(1)
                wait(peer_loaded, 32, L)
                wait(xn_ready, 2, L)
                dve.tensor_tensor(h2[:], xn[:], bc(g2row[:], 1, TB), ALU.mult).then_inc(h2_ready.sem, 1)

                def route(c, b):
                    wait_alone(bank_empty, bank_empty.at(L, FILL["s", c, b] + 1))
                    top = range(4 * c, 4 * c + 4)
                    heads = range(2 * c, 2 * c + 2)
                    for t in top:
                        ins = dve.max(vals[:, b, t, 0:8], sc[:, b, t, :])
                    step_alone(ins)
                    for t in top:
                        ins = dve.max_index(idxs[:, b, t, 0:8], vals[:, b, t, 0:8], sc[:, b, t, :])
                    step_alone(ins)
                    for t in top:
                        ins = dve.match_replace(sc[:, b, t, :], vals[:, b, t, 0:8], sc[:, b, t, :], NEG)
                    step_alone(ins)
                    for t in top:
                        ins = dve.max(vals[:, b, t, 8:16], sc[:, b, t, :])
                    step_alone(ins)
                    for t in top:
                        ins = dve.max_index(idxs[:, b, t, 8:16], vals[:, b, t, 8:16], sc[:, b, t, :])
                    step_alone(ins)
                    v4 = vals[:, b, 4 * c:4 * c + 4].rearrange("p (h c) k -> p h c k", c=2)
                    step_alone(dve.tensor_tensor(cand[:], bc(v4[:, :, 0, :], 3, TOPK), bc(v4[:, :, 1, :], 2, TOPK), ALU.add))
                    flat = cand[:].rearrange("p h i j -> p h (i j)")
                    for h in heads:
                        ins = dve.max(best[:, b, h, 0:8], flat[:, h % 2, :])
                    step_alone(ins)
                    for h in heads:
                        ins = dve.max_index(posn[:, b, h, 0:8], best[:, b, h, 0:8], flat[:, h % 2, :])
                    step_alone(ins)
                    for h in heads:
                        ins = dve.match_replace(flat[:, h % 2, :], best[:, b, h, 0:8], flat[:, h % 2, :], NEG)
                    step_alone(ins)
                    for h in heads:
                        ins = dve.max(best[:, b, h, 8:16], flat[:, h % 2, :])
                    step_alone(ins)
                    for h in heads:
                        ins = dve.max_index(posn[:, b, h, 8:16], best[:, b, h, 8:16], flat[:, h % 2, :])
                    step_alone(ins)
                    slots = slice(2 * c * TOPK, 2 * (c + 1) * TOPK)
                    pv = posn[:, b].rearrange("p h k -> p (h k)")[:, slots]
                    dve.tensor_scalar(ab_u[:, 0, slots], pv, 4, None, ALU.logical_shift_right)
                    dve.tensor_scalar(ab_u[:, 1, slots], pv, 15, None, ALU.bitwise_and)
                    step(dve.tensor_copy(idxf[:, 4 * c:4 * c + 4], idxs[:, b, 4 * c:4 * c + 4]))
                    step(dve.tensor_copy(ab_f[:, :, slots], ab_u[:, :, slots]))
                    i4 = idxf[:, 4 * c:4 * c + 4].rearrange("p (h c) k -> p h c k", c=2)
                    for half in range(2):
                        step(dve.tensor_tensor(eq[:].rearrange("p h k j -> p (h k) j"), bc(ab_f[:, half, slots], 2, TOPK),
                                               bc(const("iota"), 1, 2 * TOPK), ALU.is_equal))
                        step(dve.tensor_tensor(eq[:], eq[:], bc(i4[:, :, half, :], 2, TOPK), ALU.mult))
                        step(dve.tensor_reduce(selv[:, half, slots], eq[:].rearrange("p h k j -> p (h k) j"), AX.X, ALU.add))
                    step(dve.scalar_tensor_tensor(out=selv[:, 0, slots], in0=selv[:, 0, slots], scalar=float(PK),
                                                  in1=selv[:, 1, slots], op0=ALU.mult, op1=ALU.add))
                    dve.tensor_scalar(ex_i[:, b, slots], selv[:, 0, slots], param("row0"), None, ALU.add)\
                        .then_inc(experts_ready.sem, 1)

                def shift(b):
                    dve.tensor_tensor(gate_w[:, b], best[:, b], best[:, b, :, 0:1].broadcast_to([P, PH, TOPK]),
                                      ALU.subtract).then_inc(best_shift.sem, 1)

                def softmax(b):
                    wait(best_exp, b + 1, L)
                    step(dve.tensor_reduce(gsum[:, b], gate_w[:, b], AX.X, ALU.add))
                    step(dve.reciprocal(gsum[:, b], gsum[:, b]))
                    step_alone(dve.tensor_tensor(gate_w[:, b], gate_w[:, b], bc(gsum[:, b], 2, TOPK), ALU.mult))

                def dots(b, w):
                    for q in range(QUADS):
                        dve.wait_ge(gathered[q].sem, gathered[q].at(L, 16 * QUAD * (WAVES * 2 * b + w + 1)))
                        for s in range(QUAD):
                            row = ring[:, QUAD * q + s, :]
                            ins = dve.scalar_tensor_tensor(out=row, in0=row, scalar=1.0, in1=h2[:, b, :],
                                                           op0=ALU.mult, op1=ALU.mult,
                                                           accum_out=act_u[:, b, bass.ds(RING * w + QUAD * q + s, 1)])
                        ins.then_inc(quad_free.sem, 1)

                def add_rows(b, w):
                    for q in range(QUADS):
                        n = QUADS * (WAVES * (2 * b + 1) + w) + q
                        dve.wait_ge(gathered[q].sem, gathered[q].at(L, 16 * QUAD * (WAVES * (2 * b + 1) + w + 1)))
                        dve.wait_ge(quad_free.sem, quad_free.at(L, n))
                        dve.scalar_tensor_tensor(out=acc_v[:], in0=ring[:, QUAD * q + 3, :],
                                                 scalar=wgt[:, b, bass.ds(RING * w + QUAD * q + 3, 1)],
                                                 in1=acc_v[:], op0=ALU.mult, op1=ALU.add).then_inc(quad_free.sem, 1)

                for b in range(TB):
                    if b == 0:
                        route(0, 0)
                        route(1, 0)
                        dots(0, 0)
                        dots(0, 1)
                        route(2, 0)
                        with dve.Fori(2, 4) as w:
                            dots(0, w)
                        route(3, 0)
                        shift(0)
                    softmax(b)
                    with dve.Fori(4 if b == 0 else 0, WAVES) as w:
                        dots(b, w)
                    wait_alone(bank_empty, bank_empty.at(L, FILLS))
                    step(dve.memset(acc_v[:], 0.0))
                    wait(gelu_done, b + 1, L)
                    dve.tensor_tensor(wgt[:, b, :], gel[:, b, :], gate_w[:, b].rearrange("p h k -> p (h k)"), ALU.mult)\
                        .then_inc(wgt_ready.sem, 1)
                    wait_alone(wgt_ready, wgt_ready.at(L, b + 1))
                    if b == 0:
                        for c in range(PARTS):
                            add_rows(0, c)
                            route(c, 1)
                        shift(1)
                    with dve.Fori(PARTS if b == 0 else 0, WAVES) as w:
                        add_rows(b, w)
                    wait(quad_free, QUADS * WAVES * (2 * b + 2), L)
                    wait(diag_used, 2 + 3 * QUADS * WAVES * (b + 1), L)
                    for n in range(2):
                        ins = dve.tensor_tensor(x_tok[:, b, n * 512:(n + 1) * 512], bank[4 + 2 * b + n][:],
                                                acc_v[:, n * 512:(n + 1) * 512], ALU.add)
                    ins.then_inc(x_ready.sem, 1)
                    wait_alone(x_ready, x_ready.at(L, b + 2))
                assert st.n == DVE_STEPS, st.n

            dve.wait_ge(sq_done.sem, sq_done.at(DEPTH, 1))
            dve.tensor_scalar(rms[:], ssq[:], 1.0 / DM, EPS, ALU.mult, ALU.add).then_inc(ms_ready.sem, 1)
            dve.wait_ge(rms_ready.sem, rms_ready.at(DEPTH, 1))
            dve.reciprocal(rstd[:], rms[:]).then_inc(fin_step, 1)
            dve.wait_ge(fin_step, 1)
            dve.wait_ge(peer_loaded.sem, peer_loaded.at(DEPTH, 16))
            for b in range(TB):
                ins = dve.scalar_tensor_tensor(out=h2[:, b, :], in0=x_tok[:, b, :], scalar=rstd[:, b:b + 1], in1=g2row[:],
                                               op0=ALU.mult, op1=ALU.mult)
            ins.then_inc(out_ready, 1)

        @block.gpsimd
        def _(pool):
            def wait(sig, n, L):
                pool.wait_ge(sig.sem, sig.at(L, n))

            def wait_alone(*waits):
                waits = [(sig, pool.to_reg(value)) for sig, value in waits]
                pool.wait_ge(setup_loaded, 80)
                for sig, value in waits:
                    pool.wait_ge(sig.sem, value)

            pool.wait_ge(setup_loaded, 80)
            with pool.Fori(0, DEPTH) as L:
                wait(a_ready, 1, L)
                wait(bank_full, M_ATT + 4, L)
                for g in range(GROUPS):
                    for t in range(4):
                        d, b = divmod(t, 2)
                        if g >= 1:
                            wait(f_done, 4 * (g - 1) + t + 1, L)
                        pool.tensor_tensor(a_tri[:, t], bc(tri_ge if d else tri_le, 1, HPG),
                                           bc(a_v[:, b, d * SH + HPG * g:d * SH + HPG * (g + 1)], 2, P), ALU.mult)\
                            .then_inc(atri_ready.sem, 1)

                def wave(b, table, w, half, opening):
                    n = WAVES * (2 * b + table) + w
                    pool.tensor_copy(stage[:, half, :], ex_i[:, b, bass.ds(RING * w, RING)]).then_inc(staged.sem, 1)
                    for q in range(QUADS):
                        waits = []
                        if q == 0:
                            waits.append((staged, staged.at(L, n + 1)))
                        if not (opening and b == 0 and table == 0):
                            waits.append((quad_free, quad_free.at(L, QUADS * (n - 1) + q + 1)))
                        if table == 0 and b > 0 and opening:
                            waits.append((diag_used, diag_used.at(L, 2 + 3 * (QUADS * (WAVES * b - 1) + q + 1))))
                        if table == 1 and not opening:
                            waits.append((diag_used, diag_used.at(L, 2 + 3 * (QUADS * (WAVES * b + w - 1) + q + 1))))
                        wait_alone(*waits)
                        for s in range(QUAD):
                            r = QUAD * q + s
                            pool.indirect_dma_start(ring[:, r, :], None, peer_v if table else peer_u,
                                                    bass.IndirectOffsetOnAxis(ap=stage[:, half, r:r + 1], axis=0))\
                                .then_inc(gathered[q].sem, 16)

                for b in range(TB):
                    for table in range(2):
                        if table == 0:
                            wait_alone((experts_ready, experts_ready.at(L, PARTS * b + 1)))
                        wave(b, table, 0, 0, True)
                        wave(b, table, 1, 1, False)
                        with pool.Fori(1, WAVES // 2) as i:
                            if table == 0:
                                wait_alone((experts_ready, experts_ready.at(L, PARTS * b + 1 + i)))
                            wave(b, table, 2 * i, 0, False)
                            wave(b, table, 2 * i + 1, 1, False)


DVE_STEPS = 249


def _columns(w, parts):
    d, k, n = w.shape
    return w.reshape(d, k // P, P, parts, n // parts).transpose(0, 3, 2, 1, 4).reshape(d, parts, P, -1)


def _features(v):
    return v.reshape(DEPTH, -1, P).transpose(0, 2, 1)


def _rows(v):
    return np.broadcast_to(v.reshape(DEPTH, 1, -1), (DEPTH, P, v[0].size))


def _constants():
    c = np.zeros((P, NCONST), np.float32)
    col = {k: slice(*v) for k, v in CONST.items()}
    i = np.arange(P)
    c[:, col["ident"]] = np.eye(P)
    c[:, col["tri_le"]] = i[:, None] <= i[None, :]
    c[:, col["tri_ge"]] = i[:, None] >= i[None, :]
    c[:, col["ones"]] = 1.0
    half = ROPE // 2
    prot = np.zeros((P, P), np.float32)
    freq = np.zeros(P, np.float32)
    for c0 in range(0, P, HD):
        for j in range(half):
            prot[c0 + half + j, c0 + j] = -1.0
            prot[c0 + j, c0 + half + j] = 1.0
            freq[c0 + j] = freq[c0 + half + j] = np.float32(THETA ** (-2.0 * j / ROPE))
    c[:, col["prot"]] = prot
    c[:, col["iota"]] = np.arange(TOPK)
    c[:, col["freq"]] = freq[:, None]
    return c


def kernel(x, positions, norm1_g, w_in, gate_b, diff_lam, subln_g, w_att_br, conv_w, conv_b, dt_bias, a_log, d_skip,
           ssm_norm_g, w_ssm_br, w_out, norm2_g, peer_wq, peer_keys, peer_u, peer_v, final_g):
    import concourse.bacc as bacc
    from concourse.bass_utils import run_bass_kernel_spmd

    a = {k: np.asarray(v) for k, v in dict(
        x=x, positions=positions, norm1_g=norm1_g, w_in=w_in, gate_b=gate_b, diff_lam=diff_lam, subln_g=subln_g,
        w_att_br=w_att_br, conv_w=conv_w, conv_b=conv_b, dt_bias=dt_bias, a_log=a_log, d_skip=d_skip,
        ssm_norm_g=ssm_norm_g, w_ssm_br=w_ssm_br, w_out=w_out, norm2_g=norm2_g, peer_wq=peer_wq, peer_keys=peer_keys,
        peer_u=peer_u, peer_v=peer_v, final_g=final_g).items()}
    w = a["w_in"]
    q0, v0, z0, x0, d0, g0, n = 0, 2048, 3072, 5120, 9216, 9280, 11328
    w_stream = np.concatenate([
        _columns(w[:, :, q0:v0], 4), _columns(w[:, :, v0:z0], 2), _columns(w[:, :, x0:d0], 8),
        _columns(w[:, :, g0:g0 + DM], 2), _columns(a["w_att_br"], 2), _columns(w[:, :, z0:x0], 4),
        _columns(w[:, :, g0 + DM:n], 2), _columns(a["w_ssm_br"], 4), _columns(a["w_out"], 2), _columns(a["peer_wq"], 4)], axis=1)
    conv = a["conv_w"].transpose(0, 2, 1).reshape(DEPTH, NXBC, P, CONV).transpose(0, 2, 1, 3).reshape(DEPTH, P, -1)
    skip = np.repeat(a["d_skip"], SP_, axis=1)
    lam_init = np.array([[0.8 - 0.6 * math.exp(-0.3 * l)] for l in range(DEPTH)], np.float32)
    row0 = np.array([[l * EXPERTS] for l in range(DEPTH)], np.float32)
    params = np.concatenate([
        _features(a["norm1_g"]), _features(a["norm2_g"]), _features(a["ssm_norm_g"]), conv, _features(a["conv_b"]),
        _features(a["gate_b"]), _features(a["subln_g"]), _features(skip), _rows(a["dt_bias"]), _rows(a["a_log"]),
        _rows(a["diff_lam"]), _rows(lam_init), _rows(row0)], axis=2)
    arrays = {
        "x": a["x"],
        "positions": a["positions"],
        "consts": _constants(),
        "params": params,
        "w_stream": w_stream.reshape(DEPTH * CHUNKS, P, 4096),
        "w_dt": _columns(w[:, :, d0:g0], 1)[:, 0],
        "keys_t": a["peer_keys"].reshape(DEPTH, 2 * PH, PK, P).transpose(0, 3, 1, 2).reshape(DEPTH, P, 2 * PH * PK),
        "norm2_rows": a["norm2_g"],
        "final_row": a["final_g"].reshape(1, DM),
        "peer_u": a["peer_u"].reshape(DEPTH * EXPERTS, DM),
        "peer_v": a["peer_v"].reshape(DEPTH * EXPERTS, DM),
    }
    nc = bacc.Bacc("TRN2", target_bir_lowering=False, num_devices=1)
    ins, maps = [], {}
    for name, v in arrays.items():
        v = np.ascontiguousarray(v)
        maps[f"in_{name}"] = v
        ins.append(nc.dram_tensor(f"in_{name}", v.shape, mybir.dt.from_np(v.dtype), kind="ExternalInput").ap())
    out = nc.dram_tensor("out", (1, SEQ, DM), F32, kind="ExternalOutput").ap()
    encoder_kernel(nc, *ins, out)
    r = run_bass_kernel_spmd(nc, [maps], core_ids=[0])
    return r.results[0]["out"]
```
